# Optimizing a Trainium2 kernel written in Bass

```python
import math
import jax, jax.numpy as jnp
from jax import lax
import numpy as np

D_MODEL = 1024
BATCH = 1
SEQ = 256
DEPTH = 2

N_MIXERS = 2
N_CONV_LAYERS = (DEPTH + 1) // 2
N_ATTN_LAYERS = DEPTH // 2
D_FF = 2816
CONV_WIDTH = 3
HEAD_DIM = 64
N_Q_HEADS = D_MODEL // HEAD_DIM
N_KV_HEADS = 4
GROUP = N_Q_HEADS // N_KV_HEADS
WINDOW = 128
BLOCK = 128
ROPE_THETA = 10000.0
RMS_EPS = 1e-6

kernel_name = "hybrid_shortconv_swa_sink_macaron"

def rmsnorm(x, g):
    x32 = x.astype(jnp.float32)
    y = x32 * lax.rsqrt(jnp.mean(x32 * x32, axis=-1, keepdims=True) + RMS_EPS)
    return y.astype(x.dtype) * g

def swiglu(x, w_in, w_out):
    gate, up = jnp.split(x @ w_in, 2, axis=-1)
    return (jax.nn.silu(gate) * up) @ w_out

def short_conv_mixer(h, w_in, conv_k, w_out):
    S = h.shape[1]
    gate_b, gate_c, u = jnp.split(h @ w_in, 3, axis=-1)
    z = gate_c * u
    zp = jnp.pad(z, ((0, 0), (CONV_WIDTH - 1, 0), (0, 0)))
    conv = conv_k[0] * zp[:, 0:S]
    for tap in range(1, CONV_WIDTH):
        conv = conv + conv_k[tap] * zp[:, tap:tap + S]
    return (gate_b * conv) @ w_out

def rope_tables(positions, dtype):
    inv_freq = ROPE_THETA ** (-jnp.arange(0, HEAD_DIM, 2, dtype=jnp.float32) / HEAD_DIM)
    ang = positions.astype(jnp.float32)[..., None] * inv_freq
    return jnp.cos(ang)[:, :, None, :].astype(dtype), jnp.sin(ang)[:, :, None, :].astype(dtype)

def apply_rope(t, cos, sin):
    t1, t2 = jnp.split(t, 2, axis=-1)
    return jnp.concatenate([t1 * cos - t2 * sin, t2 * cos + t1 * sin], axis=-1)

def banded_keys(t, nb):
    B = t.shape[0]
    tb = t.reshape(B, nb, BLOCK, N_KV_HEADS, HEAD_DIM)
    prev = jnp.concatenate([jnp.zeros_like(tb[:, :1]), tb[:, :-1]], axis=1)
    return jnp.concatenate([prev, tb], axis=2)

def sliding_window_attention(h, positions, w_qkv, sinks, w_o):
    B, S, _ = h.shape
    nb = S // BLOCK
    qkv = h @ w_qkv
    q, k, v = jnp.split(qkv, [N_Q_HEADS * HEAD_DIM, (N_Q_HEADS + N_KV_HEADS) * HEAD_DIM], axis=-1)
    q = q.reshape(B, S, N_Q_HEADS, HEAD_DIM)
    k = k.reshape(B, S, N_KV_HEADS, HEAD_DIM)
    v = v.reshape(B, S, N_KV_HEADS, HEAD_DIM)
    cos, sin = rope_tables(positions, h.dtype)
    q = apply_rope(q, cos, sin)
    k = apply_rope(k, cos, sin)

    qb = q.reshape(B, nb, BLOCK, N_KV_HEADS, GROUP, HEAD_DIM)
    kw = banded_keys(k, nb)
    vw = banded_keys(v, nb)
    scale = 1.0 / math.sqrt(HEAD_DIM)
    s = jnp.einsum('bnqkgd,bnskd->bnkgqs', qb, kw).astype(jnp.float32) * scale

    qi = jnp.arange(BLOCK)[:, None]
    kj = jnp.arange(2 * BLOCK)[None, :]
    dist = qi + BLOCK - kj
    in_band = (dist >= 0) & (dist < WINDOW)
    blk = jnp.arange(nb)[:, None, None]
    mask = in_band[None] & ((blk > 0) | (kj >= BLOCK)[None])
    s = jnp.where(mask[None, :, None, None], s, jnp.finfo(jnp.float32).min)

    sink = jnp.broadcast_to(sinks.astype(jnp.float32).reshape(1, 1, N_KV_HEADS, GROUP, 1, 1),
                            s.shape[:-1] + (1,))
    p = jax.nn.softmax(jnp.concatenate([s, sink], axis=-1), axis=-1)[..., :-1].astype(h.dtype)
    o = jnp.einsum('bnkgqs,bnskd->bnqkgd', p, vw).reshape(B, S, N_Q_HEADS * HEAD_DIM)
    return o @ w_o

def setup_inputs(seed: int = 0) -> dict:
    key = jax.random.key(seed)
    ks = jax.random.split(key, 20)
    D, F = D_MODEL, D_FF
    qkv_w = (N_Q_HEADS + 2 * N_KV_HEADS) * HEAD_DIM

    def nrm(k, shape, fan_in):
        return jax.random.normal(k, shape, jnp.float32) * (fan_in ** -0.5)

    def gain(k, shape):
        return 1.0 + 0.05 * jax.random.normal(k, shape, jnp.float32)

    x = jax.random.normal(ks[0], (BATCH, SEQ, D), jnp.float32)
    positions = jnp.broadcast_to(jnp.arange(SEQ, dtype=jnp.int32)[None, :], (BATCH, SEQ))
    return {
        "x": x,
        "positions": positions,
        "ln_ff1": gain(ks[1], (DEPTH, D)),
        "w_ff1_in": nrm(ks[2], (DEPTH, D, 2 * F), D),
        "w_ff1_out": nrm(ks[3], (DEPTH, F, D), F),
        "ln_mix": gain(ks[4], (DEPTH, D)),
        "ln_ff2": gain(ks[5], (DEPTH, D)),
        "w_ff2_in": nrm(ks[6], (DEPTH, D, 2 * F), D),
        "w_ff2_out": nrm(ks[7], (DEPTH, F, D), F),
        "conv_w_in": nrm(ks[8], (N_CONV_LAYERS, D, 3 * D), D),
        "conv_kernel": nrm(ks[9], (N_CONV_LAYERS, CONV_WIDTH, D), CONV_WIDTH),
        "conv_w_out": nrm(ks[10], (N_CONV_LAYERS, D, D), D),
        "attn_w_qkv": nrm(ks[11], (N_ATTN_LAYERS, D, qkv_w), D),
        "attn_sinks": 0.5 * jax.random.normal(ks[12], (N_ATTN_LAYERS, N_Q_HEADS), jnp.float32),
        "attn_w_o": nrm(ks[13], (N_ATTN_LAYERS, N_Q_HEADS * HEAD_DIM, D), N_Q_HEADS * HEAD_DIM),
        "ln_final": gain(ks[14], (D,)),
    }

def reference(x, positions, ln_ff1, w_ff1_in, w_ff1_out, ln_mix, ln_ff2, w_ff2_in, w_ff2_out,
              conv_w_in, conv_kernel, conv_w_out, attn_w_qkv, attn_sinks, attn_w_o, ln_final):
    for i in range(DEPTH):
        x = x + 0.5 * swiglu(rmsnorm(x, ln_ff1[i]), w_ff1_in[i], w_ff1_out[i])
        h = rmsnorm(x, ln_mix[i])
        j = i // N_MIXERS
        if i % N_MIXERS == 0:
            x = x + short_conv_mixer(h, conv_w_in[j], conv_kernel[j], conv_w_out[j])
        else:
            x = x + sliding_window_attention(h, positions, attn_w_qkv[j], attn_sinks[j], attn_w_o[j])
        x = x + 0.5 * swiglu(rmsnorm(x, ln_ff2[i]), w_ff2_in[i], w_ff2_out[i])
    return rmsnorm(x, ln_final)


_drawn_inputs = setup_inputs


def setup_inputs(seed=0):
    import zlib

    import numpy as np

    out = dict(_drawn_inputs(seed))
    spreads = {}
    factors = {'attn_sinks': 8.0}
    for name, (base, spread) in spreads.items():
        noise = np.random.default_rng([zlib.crc32(name.encode()), seed]).standard_normal(out[name].shape)
        drawn = base * np.exp(spread * noise) if base else spread * noise
        out[name] = __import__('jax').numpy.asarray(drawn.astype(out[name].dtype))
    for name, factor in factors.items():
        out[name] = (out[name] * factor).astype(out[name].dtype)
    return out
```

```python
from contextlib import ExitStack
import math

import numpy as np

import concourse.bass as bass
from concourse import mybir

F32 = mybir.dt.float32
F32R = mybir.dt.float32r
I32 = mybir.dt.int32
ALU = mybir.AluOpType
ACT = mybir.ActivationFunctionType
AX = mybir.AxisListType

P = 128
D = 1024
SEQ = 256
NT = SEQ // P
KD = D // P
F = 2816
UNIT = 256
NJ = F // UNIT
W = 512
HALF = KD // 2
HD = 64
NKV = 4
NQ = 16
EPS = 1e-6
THETA = 10000.0
NEG = -3.4028234663852886e38

FF, CONV, ATTN = "ff", "conv", "attn"
STAGES = [FF, CONV, FF, FF, ATTN, FF]
IN_UNITS = {FF: NJ, CONV: 3 * D // W, ATTN: (NQ + 2 * NKV) * HD // W}
OUT_UNITS = {FF: NJ, CONV: D // UNIT, ATTN: D // UNIT}
IN_BASE = [sum(IN_UNITS[k] for k in STAGES[:s]) for s in range(len(STAGES) + 1)]
OUT_BASE = [sum(OUT_UNITS[k] for k in STAGES[:s]) for s in range(len(STAGES) + 1)]
FF_INDEX = {0: 0, 2: 1, 3: 2, 5: 3}
MIX_INDEX = {1: 0, 4: 1}
PIECES = 4
LOOP_FROM, LOOP_TURNS = 2, 4

CONV_COLS = [D, 2 * D, D + W, 2 * D + W, 0, W]
ATTN_COLS = [NQ * HD, 0, W]

GAIN_ROWS = len(STAGES) * KD
CONV_ROWS = 3 * KD


def two_pi_parts(count, bits):
    parts, rest = [], 2 * math.pi
    for _ in range(count - 1):
        _, e = math.frexp(rest)
        step = 2.0 ** (e - bits)
        part = math.floor(rest / step) * step
        parts.append(part)
        rest -= part
    return parts + [rest]


def attention_group(g):
    chunk, r = divmod(g, 6)
    if r < 2:
        return 0, list(range(8 * chunk + r, 8 * chunk + 8, 2))
    first = 8 * chunk + (0, 1, 4, 5)[r - 2]
    return 1, [first, first + 2]


GROUPS = 12
BATCH_LAST = {1: 0, 5: 1, 7: 2, 11: 3}


def exps_through(g):
    return sum(len(attention_group(n)[1]) for n in range(g + 1))


def rope_writes(n):
    return 4 * n if n <= 2 else 8 + 2 * (n - 2)


def build(nc, x_in, positions, ln_ff1, w_ff1_in, w_ff1_out, ln_mix, ln_ff2, w_ff2_in, w_ff2_out,
          conv_w_in, conv_kernel, conv_w_out, attn_w_qkv, attn_sinks, attn_w_o, ln_final,
          inv_freq, out):
    w_in = {0: w_ff1_in[0], 1: conv_w_in[0], 2: w_ff2_in[0], 3: w_ff1_in[1], 4: attn_w_qkv[0], 5: w_ff2_in[1]}
    w_out = {0: w_ff1_out[0], 1: conv_w_out[0], 2: w_ff2_out[0], 3: w_ff1_out[1], 4: attn_w_o[0], 5: w_ff2_out[1]}
    gains = [ln_ff1[0], ln_mix[0], ln_ff2[0], ln_ff1[1], ln_mix[1], ln_ff2[1]]

    with ExitStack() as ctx:
        def sb(name, shape, dt=F32):
            return ctx.enter_context(nc.sbuf_tensor(name, shape, dt))

        def sem(name):
            return ctx.enter_context(nc.semaphore(name))

        raw_in = sb("raw_in", [P, KD, W])
        raw_out = sb("raw_out", [P, 2, D])
        in_hi = sb("in_hi", [P, 2, KD, W], F32R)
        in_lo = sb("in_lo", [P, 2, KD, W], F32R)
        out_hi = sb("out_hi", [P, 2, 2, D], F32R)
        out_lo = sb("out_lo", [P, 2, 2, D], F32R)
        x = sb("x", [P, NT, D])
        xT_hi = sb("xT_hi", [P, KD, SEQ], F32R)
        xT_lo = sb("xT_lo", [P, KD, SEQ], F32R)
        hT_hi = sb("hT_hi", [P, 2, 2, SEQ], F32R)
        hT_lo = sb("hT_lo", [P, 2, 2, SEQ], F32R)
        y_hi = sb("y_hi", [P, KD, SEQ], F32R)
        y_lo = sb("y_lo", [P, KD, SEQ], F32R)
        pair = sb("pair", [P, 2, W])
        gated = sb("gated", [P, 2 * W])
        scratch = sb("scratch", [P, 6656])
        ident = sb("ident", [P, P])
        band = sb("band", [P, 2 * P])
        rows = sb("rows", [GAIN_ROWS + CONV_ROWS, P])
        cols = sb("cols", [P, GAIN_ROWS + CONV_ROWS])
        sink = sb("sink", [P, NQ])
        neg_sink = sb("neg_sink", [P, NQ])
        freq = sb("freq", [P, HD // 2])
        pos_i = sb("pos_i", [P, NT], I32)
        pos_f = sb("pos_f", [P, NT])
        angle = sb("angle", [P, NT, HD // 2])
        turns = sb("turns", [P, NT, HD // 2])
        sin_t = sb("sin_t", [P, NT, HD // 2])
        cos_t = sb("cos_t", [P, NT, HD // 2])
        sq_sum = sb("sq_sum", [P, 2 * 7])
        mean_sq = sb("mean_sq", [P, 2 * 7])
        rstd = sb("rstd", [P, 2 * 7])
        minus_half = sb("minus_half", [P, 1])
        neg_max = sb("neg_max", [P, NT, NQ])
        sink_arg = sb("sink_arg", [P, NT, NQ])
        sink_exp = sb("sink_exp", [P, NT, NQ])
        prob_sum = sb("prob_sum", [P, NT, NQ])
        denom = sb("denom", [P, NT, NQ])
        inv_denom = sb("inv_denom", [P, NT, NQ])

        silu_buf = gated[:, 0:W].rearrange("p (t n) -> p t n", t=NT)
        hid_buf = gated[:, W:2 * W].rearrange("p (t n) -> p t n", t=NT)
        rope_cos = gated[:, 0:W]
        rope_sin = gated[:, W:2 * W]

        c_tok = scratch[:, 0:1024].rearrange("p (t n) -> p t n", t=NT)
        z_tok = scratch[:, 1024:2048].rearrange("p (t n) -> p t n", t=NT)
        PAD = SEQ + 2
        z_feat = scratch[:, 2048:2048 + KD * PAD].rearrange("p (k n) -> p k n", k=KD)
        conv_at = 2048 + KD * PAD
        conv_buf = scratch[:, conv_at:conv_at + KD * SEQ].rearrange("p (k n) -> p k n", k=KD)
        q_tok = scratch[:, 0:1024].rearrange("p (t n) -> p t n", t=NT)
        kd_tok = scratch[:, 1024:2048].rearrange("p (t n) -> p t n", t=NT)
        o_tok = kd_tok
        v_tok = scratch[:, 2048:2560].rearrange("p (t n) -> p t n", t=NT)
        qT = scratch[:, 2560:4608].rearrange("p (h n) -> p h n", h=NQ // 2)
        kT = scratch[:, 4608:5632].rearrange("p (h n) -> p h n", h=NKV)
        pT = scratch[:, 5632:6656].rearrange("p (s n) -> p s n", s=2)
        g_fin = scratch[:, 0:D]
        fin = scratch[:, D:3 * D].rearrange("p (t n) -> p t n", t=NT)

        acc = [[ctx.enter_context(nc.psum_tensor(f"acc{t}{h}", [P, W], F32)) for h in range(2)] for t in range(NT)]
        proj = [ctx.enter_context(nc.psum_tensor(f"proj{t}", [P, W], F32)) for t in range(NT)]
        tp = [ctx.enter_context(nc.psum_tensor(f"tp{i}", [P, W], F32)) for i in range(2)]
        tp4 = [b[:, :].rearrange("p (k n) -> p k n", k=HALF) for b in tp]
        scores = acc[0]
        pT_ps = acc[1][0]
        o_ps = acc[1][1]

        x_landed = [sem(f"x_landed{t}") for t in range(NT)]
        rows_landed = sem("rows_landed")
        pos_landed = sem("pos_landed")
        g_fin_landed = sem("g_fin_landed")
        in_landed = [sem(f"in_landed{h}") for h in range(2)]
        out_landed = [sem(f"out_landed{h}") for h in range(2)]
        in_hi_done = sem("in_hi_done")
        in_lo_done = sem("in_lo_done")
        out_hi_done = sem("out_hi_done")
        out_lo_done = sem("out_lo_done")
        proj_done = sem("proj_done")
        out_used = sem("out_used")
        acc_first = sem("acc_first")
        x_ready = sem("x_ready")
        xT_ps = sem("xT_ps")
        gained = sem("gained")
        xT_hi_done = sem("xT_hi_done")
        xT_lo_done = sem("xT_lo_done")
        sq_ready = sem("sq_ready")
        mean_ready = sem("mean_ready")
        rstd_ready = sem("rstd_ready")
        silu_done = sem("silu_done")
        h_ready = sem("h_ready")
        hT_ps = sem("hT_ps")
        hT_hi_done = sem("hT_hi_done")
        hT_lo_done = sem("hT_lo_done")
        ident_ready = sem("ident_ready")
        consts_ready = sem("consts_ready")
        cols_ps = sem("cols_ps")
        cols_ready = sem("cols_ready")
        vec_step = sem("vec_step")
        trig_arg = sem("trig_arg")
        trig_ready = sem("trig_ready")
        pads_ready = sem("pads_ready")
        c_ready = sem("c_ready")
        z_ready = sem("z_ready")
        z_ps = sem("z_ps")
        z_feat_ready = sem("z_feat_ready")
        conv_step = sem("conv_step")
        b_ps = sem("b_ps")
        y_f_ready = sem("y_f_ready")
        y_hi_done = sem("y_hi_done")
        y_lo_done = sem("y_lo_done")
        tables_ready = sem("tables_ready")
        v_ready = sem("v_ready")
        rope_ab = sem("rope_ab")
        rope_out = sem("rope_out")
        qk_ps = sem("qk_ps")
        qkT_ready = sem("qkT_ready")
        scores_done = sem("scores_done")
        masked = sem("masked")
        max_step = sem("max_step")
        neg_max_ready = sem("neg_max_ready")
        exp_done = sem("exp_done")
        sink_exp_done = sem("sink_exp_done")
        probT_ps = sem("probT_ps")
        probT_ready = sem("probT_ready")
        pv_done = sem("pv_done")
        den_step = sem("den_step")
        o_ready = sem("o_ready")
        o_ps_T = sem("o_ps_T")
        fin_ready = sem("fin_ready")
        stored = sem("stored")

        def gain_of(m, half):
            return cols[:, m * KD + half * HALF:m * KD + (half + 1) * HALF].unsqueeze(2).to_broadcast([P, HALF, P])

        block = ctx.enter_context(nc.Block())

        @block.sync
        def _(sp):
            def load_in(u, s, col_a, col_b):
                src = w_in[s].rearrange("(k p) n -> p k n", p=P)
                for h in range(2):
                    if not isinstance(u, int) or u >= 1:
                        sp.wait_ge(in_lo_done, PIECES * (u - 1) + 2 * (h + 1))
                    ks = slice(h * HALF, (h + 1) * HALF)
                    for n, col in enumerate((col_a, col_b)):
                        sp.dma_start(raw_in[:, ks, n * UNIT:(n + 1) * UNIT],
                                     src[:, ks, bass.ds(col, UNIT)]).then_inc(in_landed[h], 16)

            def load_out(o, s, row):
                for h in range(2):
                    if not isinstance(o, int) or o >= 1:
                        sp.wait_ge(out_lo_done, 2 * (o - 1) + h + 1)
                    sp.dma_start(raw_out[:, h, :], w_out[s][bass.ds(row + h * P, P), :]).then_inc(out_landed[h], 16)

            def first_in(s):
                if s == len(STAGES):
                    return
                col = {FF: 0, CONV: CONV_COLS[0], ATTN: ATTN_COLS[0]}[STAGES[s]]
                load_in(IN_BASE[s], s, col, F if STAGES[s] == FF else col + UNIT)

            for t in range(NT):
                sp.dma_start(x[:, t, :], x_in[0, t * P:(t + 1) * P, :]).then_inc(x_landed[t], 16)
            for m in range(len(STAGES)):
                sp.dma_start(rows[m * KD:(m + 1) * KD, :], gains[m].rearrange("(k p) -> k p", p=P)).then_inc(rows_landed, 16)
            sp.dma_start(rows[GAIN_ROWS:GAIN_ROWS + CONV_ROWS, :],
                         conv_kernel[0].rearrange("w (k p) -> (w k) p", p=P)).then_inc(rows_landed, 16)
            first_in(0)
            sp.dma_start(sink[:, :], attn_sinks[0].partition_broadcast(P)).then_inc(pos_landed, 16)
            sp.dma_start(freq[:, :], inv_freq).then_inc(pos_landed, 16)
            with nc.allow_non_contiguous_dma(reason="256 positions, four bytes each"):
                sp.dma_start(pos_i[:, :], positions[0].rearrange("(t p) -> p t", p=P)).then_inc(pos_landed, 16)

            for s, kind in enumerate(STAGES):
                u, o = IN_BASE[s], OUT_BASE[s]
                if kind == FF:
                    load_in(u + 1, s, UNIT, F + UNIT)
                    load_out(o, s, 0)
                    with sp.Fori(1, NJ - 1) as j:
                        load_in(u + 1 + j, s, (j + 1) * UNIT, (j + 1) * UNIT + F)
                        load_out(o + j, s, j * UNIT)
                    first_in(s + 1)
                    load_out(o + NJ - 1, s, (NJ - 1) * UNIT)
                elif kind == CONV:
                    for q in (1, 2, 3, "out0", 4, 5, "out1"):
                        if isinstance(q, int):
                            load_in(u + q, s, CONV_COLS[q], CONV_COLS[q] + UNIT)
                        else:
                            load_out(o + int(q[3:]), s, int(q[3:]) * UNIT)
                    first_in(s + 1)
                    load_out(o + 2, s, 2 * UNIT)
                    load_out(o + 3, s, 3 * UNIT)
                else:
                    for q in (1, 2):
                        load_in(u + q, s, ATTN_COLS[q], ATTN_COLS[q] + UNIT)
                    load_out(o, s, 0)
                    load_out(o + 1, s, UNIT)
                    first_in(s + 1)
                    load_out(o + 2, s, 2 * UNIT)
                    load_out(o + 3, s, 3 * UNIT)
                    sp.wait_ge(out_used, OUT_BASE[s + 1])
                    sp.dma_start(g_fin, ln_final.partition_broadcast(P)).then_inc(g_fin_landed, 16)
            for t in range(NT):
                sp.wait_ge(fin_ready, t + 1)
                sp.dma_start(out[0, t * P:(t + 1) * P, :], fin[:, t, :]).then_inc(stored, 16)
            sp.wait_ge(stored, 16 * NT)

        @block.gpsimd
        def _(pool):
            pool.memset(ident[:, :], 0.0).then_inc(ident_ready, 1)
            pool.wait_ge(ident_ready, 1)
            pool.affine_select(out=ident[:, :], in_=ident[:, :], compare_op=ALU.not_equal, fill=1.0, base=0,
                               pattern=[[-1, P]], channel_multiplier=1).then_inc(ident_ready, 1)
            pool.memset(minus_half[:, :], -0.5).then_inc(consts_ready, 1)
            pool.memset(band[:, :], 0.0).then_inc(consts_ready, 1)
            pool.wait_ge(consts_ready, 2)
            pool.affine_select(out=band[:, :], in_=band[:, :], compare_op=ALU.is_ge, fill=NEG, base=-1,
                               pattern=[[1, 2 * P]], channel_multiplier=-1).then_inc(consts_ready, 1)
            pool.wait_ge(consts_ready, 3)
            pool.affine_select(out=band[:, :], in_=band[:, :], compare_op=ALU.is_ge, fill=NEG, base=P,
                               pattern=[[-1, 2 * P]], channel_multiplier=1).then_inc(consts_ready, 1)
            pool.memset(z_feat[:, :, 0:2], 0.0).then_inc(pads_ready, 1)

            def rope_sums(n):
                heads = NKV if n < 2 else 8
                a = rope_cos[:, 0:heads * HD].rearrange("p (h e d) -> p h e d", h=heads, e=2)
                b = rope_sin[:, 0:heads * HD].rearrange("p (h e d) -> p h e d", h=heads, e=2)
                pool.wait_ge(rope_ab, n + 1)
                if n >= 4:
                    pool.wait_ge(qk_ps, n - 1)
                if n < 2:
                    dst = kd_tok[:, n, :].rearrange("p (h c e d) -> p c h e d", h=heads, c=2, e=2)
                    dsts = [dst[:, 0], dst[:, 1]]
                else:
                    dsts = [q_tok[:, n % 2, :].rearrange("p (h e d) -> p h e d", h=heads, e=2)]
                for to in dsts:
                    pool.tensor_tensor(to[:, :, 0, :], a[:, :, 0, :], b[:, :, 1, :], ALU.subtract).then_inc(rope_out, 1)
                    pool.tensor_tensor(to[:, :, 1, :], a[:, :, 1, :], b[:, :, 0, :], ALU.add).then_inc(rope_out, 1)

            for m in range(len(STAGES) + 1):
                for t in range(NT):
                    i = 2 * m + t
                    pool.wait_ge(sq_ready, i + 1)
                    pool.tensor_scalar(mean_sq[:, i:i + 1], sq_sum[:, i:i + 1], 1.0 / D, EPS,
                                       ALU.mult, ALU.add).then_inc(mean_ready, 1)
                    pool.wait_ge(mean_ready, i + 1)
                    pool.tensor_tensor(rstd[:, i:i + 1], mean_sq[:, i:i + 1], minus_half[:, :],
                                       ALU.pow).then_inc(rstd_ready, 1)
                if m < len(STAGES) and STAGES[m] == ATTN:
                    for n in range(6):
                        rope_sums(n)

        @block.scalar
        def _(act):
            def split_in(u, slot, pieces):
                for q in pieces:
                    act.wait_ge(in_landed[q // 2], 32 * (u + 1))
                    if q == 0 and (not isinstance(u, int) or u >= 2):
                        act.wait_ge(proj_done, 2 * (u - 1))
                    act.activation(in_hi[:, slot, 2 * q:2 * q + 2, :], raw_in[:, 2 * q:2 * q + 2, :],
                                   ACT.Copy).then_inc(in_hi_done, 1)

            def split_out(o, slot, halves=(0, 1)):
                for h in halves:
                    act.wait_ge(out_landed[h], 16 * (o + 1))
                    if h == 0 and (not isinstance(o, int) or o >= 2):
                        act.wait_ge(out_used, o - 1)
                    act.activation(out_hi[:, slot, h, :], raw_out[:, h, :], ACT.Copy).then_inc(out_hi_done, 1)

            def norm_hi(m, t):
                for half in range(2):
                    act.wait_ge(gained, 4 * m + 2 * t + half + 1)
                    act.activation(xT_hi[:, half * HALF:(half + 1) * HALF, t * P:(t + 1) * P],
                                   pair[:, half, :].rearrange("p (k n) -> p k n", k=HALF),
                                   ACT.Copy).then_inc(xT_hi_done, 1)

            def squares(m, t):
                if m == 0:
                    act.wait_ge(x_landed[t], 16)
                else:
                    act.wait_ge(x_ready, 4 * (m - 1) + 2 * t + 2)
                i = 2 * m + t
                if i >= 1:
                    act.wait_ge(sq_ready, i)
                act.activation(gated[:, :], x[:, t, :], ACT.Square, accum_out=sq_sum[:, i:i + 1]).then_inc(sq_ready, 1)

            def silu(c, u, t, first_of=None):
                act.wait_ge(proj_done, 2 * u + t + 1)
                if first_of is not None:
                    act.wait_ge(rstd_ready, 2 * first_of + t + 1)
                    act.wait_ge(sq_ready, 2 * first_of + 2)
                act.activation(silu_buf[:, t, :], proj[t][:, 0:UNIT], ACT.Silu,
                               scale=rstd_col[0][:, t:t + 1]).then_inc(silu_done, 1)

            def hidden_hi(c, slot):
                act.wait_ge(hT_ps, c + 1)
                act.activation(hT_hi[:, slot, :, :].rearrange("p k n -> p (k n)"), tp[0][:, :],
                               ACT.Copy).then_inc(hT_hi_done, 1)

            rstd_col = [None]
            act.wait_ge(trig_arg, 1)
            act.activation(sin_t[:, :, :], angle[:, :, :], ACT.Sin).then_inc(trig_ready, 1)
            act.activation(cos_t[:, :, :], turns[:, :, :], ACT.Sin).then_inc(trig_ready, 1)
            squares(0, 0)
            split_in(0, 0, (0, 1))
            norm_hi(0, 0)
            squares(0, 1)
            split_in(0, 0, (2, 3))
            norm_hi(0, 1)

            for s, kind in enumerate(STAGES):
                u, o, m = IN_BASE[s], OUT_BASE[s], s
                rstd_col[0] = rstd[:, 2 * m:2 * m + 2]
                next_u = IN_BASE[s + 1] if s + 1 < len(STAGES) else None
                if kind == FF:
                    c = NJ * FF_INDEX[s]
                    split_in(u + 1, (u + 1) % 2, (0, 1))
                    silu(c, u, 0, m)
                    split_in(u + 1, (u + 1) % 2, (2, 3))
                    silu(c, u, 1, m)
                    split_out(o, o % 2)

                    def middle(j, par):
                        silu(c + j, u + j, 0)
                        hidden_hi(c + j - 1, (c + par + 1) % 2)
                        split_in(u + j + 1, (u + par + 1) % 2, (0, 1, 2))
                        silu(c + j, u + j, 1)
                        split_in(u + j + 1, (u + par + 1) % 2, (3,))
                        split_out(o + j, (o + par) % 2)

                    middle(1, 1)
                    with act.Fori(0, LOOP_TURNS) as i:
                        for b in range(2):
                            middle(LOOP_FROM + 2 * i + b, b)
                    j = NJ - 1
                    silu(c + j, u + j, 0)
                    hidden_hi(c + j - 1, (c + j - 1) % 2)
                    split_out(o + j, (o + j) % 2)
                    if next_u:
                        split_in(next_u, next_u % 2, (0,))
                    silu(c + j, u + j, 1)
                    hidden_hi(c + j, (c + j) % 2)
                    if next_u:
                        split_in(next_u, next_u % 2, (1, 2, 3))
                elif kind == CONV:
                    def c_rows(n, q, t):
                        act.wait_ge(proj_done, 2 * (u + q) + t + 1)
                        if n == 0:
                            act.wait_ge(rstd_ready, 2 * m + t + 1)
                        if 1 <= n <= 2:
                            act.wait_ge(z_ready, 2 * (n - 1) + t + 1)
                        if n == 3:
                            act.wait_ge(b_ps, t + 1)
                        act.activation(c_tok[:, t, :], proj[t][:, :], ACT.Copy,
                                       scale=rstd_col[0][:, t:t + 1]).then_inc(c_ready, 1)

                    def z_to_features(half, t):
                        act.wait_ge(z_ps, 2 * half + t + 1)
                        act.activation(z_feat[:, half * HALF:(half + 1) * HALF, 2 + t * P:2 + (t + 1) * P],
                                       tp4[t], ACT.Copy).then_inc(z_feat_ready, 1)

                    def y_hi_conv(half, t):
                        act.wait_ge(y_f_ready, 2 * half + t + 1)
                        act.activation(y_hi[:, half * HALF:(half + 1) * HALF, t * P:(t + 1) * P],
                                       pair[:, t, :].rearrange("p (k n) -> p k n", k=HALF),
                                       ACT.Copy).then_inc(y_hi_done, 1)

                    def unit(q, pieces):
                        split_in(u + q, (u + q) % 2, pieces)

                    unit(1, (0, 1))
                    c_rows(0, 0, 0)
                    unit(1, (2, 3))
                    c_rows(0, 0, 1)
                    unit(2, (0, 1, 2, 3))
                    unit(3, (0, 1))
                    c_rows(1, 2, 0)
                    z_to_features(0, 0)
                    z_to_features(0, 1)
                    unit(3, (2, 3))
                    c_rows(1, 2, 1)
                    split_out(o, o % 2)
                    unit(4, (0, 1, 2, 3))
                    unit(5, (0, 1))
                    c_rows(2, 4, 0)
                    z_to_features(1, 0)
                    z_to_features(1, 1)
                    unit(5, (2, 3))
                    c_rows(2, 4, 1)
                    split_out(o + 1, (o + 1) % 2)
                    split_in(next_u, next_u % 2, (0, 1))
                    y_hi_conv(0, 0)
                    c_rows(3, 5, 0)
                    y_hi_conv(0, 1)
                    split_in(next_u, next_u % 2, (2, 3))
                    c_rows(3, 5, 1)
                    y_hi_conv(1, 0)
                    y_hi_conv(1, 1)
                    split_out(o + 2, (o + 2) % 2)
                    split_out(o + 3, (o + 3) % 2)
                else:
                    def v_rows(t):
                        act.wait_ge(proj_done, 2 * u + t + 1)
                        act.wait_ge(rstd_ready, 2 * m + t + 1)
                        act.activation(v_tok[:, t, :], proj[t][:, 256:512], ACT.Copy,
                                       scale=rstd_col[0][:, t:t + 1]).then_inc(v_ready, 1)

                    def qk_out(n):
                        act.wait_ge(qk_ps, n + 1)
                        t = n % 2
                        to = kT[:, :, t * P:(t + 1) * P] if n < 2 else \
                            qT[:, HALF * (n // 2 - 1):HALF * (n // 2), t * P:(t + 1) * P]
                        act.activation(to, tp4[t], ACT.Copy).then_inc(qkT_ready, 1)

                    def exps(g):
                        t, heads = attention_group(g)
                        act.wait_ge(neg_max_ready, g + 1)
                        keys = W // len(heads)
                        for n, h in enumerate(heads):
                            part = pair[:, g % 2, n * keys:(n + 1) * keys]
                            act.activation(part, part, ACT.Exp, bias=neg_max[:, t, h:h + 1],
                                           accum_out=prob_sum[:, t, h:h + 1]).then_inc(exp_done, 1)
                        if g in BATCH_LAST:
                            b = BATCH_LAST[g]
                            hs = slice(8 * (b // 2), 8 * (b // 2) + 8)
                            act.activation(sink_exp[:, t, hs], sink_arg[:, t, hs], ACT.Exp).then_inc(sink_exp_done, 1)

                    def y_hi_attn(b):
                        act.wait_ge(o_ps_T, b + 1)
                        half, t = divmod(b, 2)
                        act.activation(y_hi[:, half * HALF:(half + 1) * HALF, t * P:(t + 1) * P],
                                       tp4[t], ACT.Copy).then_inc(y_hi_done, 1)

                    split_in(u + 1, (u + 1) % 2, (0, 1))
                    v_rows(0)
                    split_in(u + 1, (u + 1) % 2, (2, 3))
                    v_rows(1)
                    split_in(u + 2, (u + 2) % 2, (0, 1))
                    qk_out(0)
                    qk_out(1)
                    split_in(u + 2, (u + 2) % 2, (2, 3))
                    split_out(o, o % 2)
                    qk_out(2)
                    qk_out(3)
                    for g in range(GROUPS):
                        exps(g)
                        if g < 2:
                            split_out(o + 1, (o + 1) % 2, (g,))
                        elif g < 6:
                            split_in(next_u, next_u % 2, (g - 2,))
                        if g == 4:
                            y_hi_attn(0)
                        if g == 5:
                            qk_out(4)
                            qk_out(5)
                        if g == 6:
                            y_hi_attn(1)
                        if g == 10:
                            y_hi_attn(2)
                    y_hi_attn(3)
                    split_out(o + 2, (o + 2) % 2)
                    split_out(o + 3, (o + 3) % 2)
                for t in range(NT):
                    if s + 1 < len(STAGES):
                        norm_hi(m + 1, t)
                    squares(m + 1, t)

        @block.vector
        def _(dve):
            steps = [0]

            def step(instruction):
                instruction.then_inc(vec_step, 1)
                steps[0] += 1
                dve.wait_ge(vec_step, steps[0])

            def split_in(u, slot, pieces):
                for q in pieces:
                    dve.wait_ge(in_hi_done, PIECES * u + q + 1)
                    dve.tensor_tensor(in_lo[:, slot, 2 * q:2 * q + 2, :], raw_in[:, 2 * q:2 * q + 2, :],
                                      in_hi[:, slot, 2 * q:2 * q + 2, :].bitcast(F32),
                                      ALU.subtract).then_inc(in_lo_done, 1)

            def split_out(o, slot, halves=(0, 1)):
                for h in halves:
                    dve.wait_ge(out_hi_done, 2 * o + h + 1)
                    dve.tensor_tensor(out_lo[:, slot, h, :], raw_out[:, h, :], out_hi[:, slot, h, :].bitcast(F32),
                                      ALU.subtract).then_inc(out_lo_done, 1)

            def residual(m, t, scale):
                if t == 0:
                    dve.wait_ge(acc_first, m)
                else:
                    dve.wait_ge(out_used, OUT_BASE[m])
                for half in range(2):
                    part = x[:, t, half * W:(half + 1) * W]
                    dve.scalar_tensor_tensor(out=part, in0=acc[t][half][:, :], scalar=scale, in1=part,
                                             op0=ALU.mult, op1=ALU.add).then_inc(x_ready, 1)

            def norm_lo(m, t):
                for half in range(2):
                    n = 4 * m + 2 * t + half
                    dve.wait_ge(xT_ps, n + 1)
                    if n >= 2:
                        dve.wait_ge(xT_lo_done, n - 1)
                    dve.tensor_tensor(pair[:, half, :].rearrange("p (k n) -> p k n", k=HALF), tp4[half],
                                      gain_of(m, half), ALU.mult).then_inc(gained, 1)
                for half in range(2):
                    n = 4 * m + 2 * t + half
                    ks, ts = slice(half * HALF, (half + 1) * HALF), slice(t * P, (t + 1) * P)
                    dve.wait_ge(xT_hi_done, n + 1)
                    dve.tensor_tensor(xT_lo[:, ks, ts], pair[:, half, :].rearrange("p (k n) -> p k n", k=HALF),
                                      xT_hi[:, ks, ts].bitcast(F32), ALU.subtract).then_inc(xT_lo_done, 1)

            def hidden(c, t):
                dve.wait_ge(silu_done, 2 * c + t + 1)
                if not isinstance(c, int) or c >= 1:
                    dve.wait_ge(hT_ps, c)
                dve.scalar_tensor_tensor(out=hid_buf[:, t, :], in0=proj[t][:, UNIT:2 * UNIT],
                                         scalar=rstd_col[0][:, t:t + 1], in1=silu_buf[:, t, :],
                                         op0=ALU.mult, op1=ALU.mult).then_inc(h_ready, 1)

            def hidden_lo(c, slot):
                dve.wait_ge(hT_hi_done, c + 1)
                dve.tensor_tensor(hT_lo[:, slot, :, :].rearrange("p k n -> p (k n)"), tp[0][:, :],
                                  hT_hi[:, slot, :, :].rearrange("p k n -> p (k n)").bitcast(F32),
                                  ALU.subtract).then_inc(hT_lo_done, 1)

            rstd_col = [None]
            dve.wait_ge(cols_ps, 1)
            dve.tensor_copy(cols[:, :], tp[0][:, 0:GAIN_ROWS + CONV_ROWS]).then_inc(cols_ready, 1)
            dve.wait_ge(pos_landed, 48)
            step(dve.tensor_copy(pos_f[:, :], pos_i[:, :]))
            for t in range(NT):
                step(dve.tensor_scalar(angle[:, t, :], freq[:, :], pos_f[:, t:t + 1], None, ALU.mult))
            magic = 1.5 * 2.0 ** 23
            step(dve.tensor_scalar(turns[:, :, :], angle[:, :, :], 1.0 / (2 * math.pi), magic, ALU.mult, ALU.add))
            step(dve.tensor_scalar(turns[:, :, :], turns[:, :, :], -magic, None, ALU.add))
            for part in two_pi_parts(4, 8):
                step(dve.scalar_tensor_tensor(out=angle[:, :, :], in0=turns[:, :, :], scalar=-part,
                                              in1=angle[:, :, :], op0=ALU.mult, op1=ALU.add))
            top = 3.1415925
            step(dve.tensor_scalar(angle[:, :, :], angle[:, :, :], top, -top, ALU.min, ALU.max))
            step(dve.scalar_tensor_tensor(out=turns[:, :, :], in0=angle[:, :, :], scalar=-1.0,
                                          in1=angle[:, :, :], op0=ALU.mult, op1=ALU.max))
            dve.tensor_scalar(turns[:, :, :], turns[:, :, :], -1.0, math.pi / 2, ALU.mult, ALU.add).then_inc(trig_arg, 1)
            dve.tensor_scalar(neg_sink[:, :], sink[:, :], -1.0, None, ALU.mult).then_inc(vec_step, 1)
            steps[0] += 1

            dve.wait_ge(cols_ready, 1)
            split_in(0, 0, (0, 1))
            norm_lo(0, 0)
            split_in(0, 0, (2, 3))
            norm_lo(0, 1)

            for s, kind in enumerate(STAGES):
                u, o, m = IN_BASE[s], OUT_BASE[s], s
                rstd_col[0] = rstd[:, 2 * m:2 * m + 2]
                next_u = IN_BASE[s + 1] if s + 1 < len(STAGES) else None
                if kind == FF:
                    c = NJ * FF_INDEX[s]
                    split_in(u + 1, (u + 1) % 2, (0, 1))
                    hidden(c, 0)
                    split_in(u + 1, (u + 1) % 2, (2, 3))
                    hidden(c, 1)
                    split_out(o, o % 2)

                    def middle(j, par):
                        hidden(c + j, 0)
                        hidden_lo(c + j - 1, (c + par + 1) % 2)
                        split_in(u + j + 1, (u + par + 1) % 2, (0, 1, 2))
                        hidden(c + j, 1)
                        split_in(u + j + 1, (u + par + 1) % 2, (3,))
                        split_out(o + j, (o + par) % 2)

                    middle(1, 1)
                    with dve.Fori(0, LOOP_TURNS) as i:
                        for b in range(2):
                            middle(LOOP_FROM + 2 * i + b, b)
                    j = NJ - 1
                    hidden(c + j, 0)
                    hidden_lo(c + j - 1, (c + j - 1) % 2)
                    split_out(o + j, (o + j) % 2)
                    if next_u:
                        split_in(next_u, next_u % 2, (0,))
                    hidden(c + j, 1)
                    hidden_lo(c + j, (c + j) % 2)
                    if next_u:
                        split_in(next_u, next_u % 2, (1, 2, 3))
                elif kind == CONV:
                    def z_rows(half, q, t):
                        dve.wait_ge(proj_done, 2 * (u + q) + t + 1)
                        dve.wait_ge(c_ready, 2 * half + t + 1)
                        if half == 1:
                            dve.wait_ge(z_ps, t + 1)
                        dve.scalar_tensor_tensor(out=z_tok[:, t, :], in0=proj[t][:, :],
                                                 scalar=rstd_col[0][:, t:t + 1], in1=c_tok[:, t, :],
                                                 op0=ALU.mult, op1=ALU.mult).then_inc(z_ready, 1)

                    def taps(half):
                        dve.wait_ge(z_feat_ready, 2 * half + 2)
                        dve.wait_ge(pads_ready, 1)
                        for tap in range(3):
                            for n in range(HALF):
                                k = half * HALF + n
                                at = GAIN_ROWS + tap * KD + k
                                src, to = z_feat[:, k, tap:tap + SEQ], conv_buf[:, k, :]
                                if tap == 0:
                                    dve.tensor_scalar(to, src, cols[:, at:at + 1], None,
                                                      ALU.mult).then_inc(conv_step, 1)
                                else:
                                    dve.wait_ge(conv_step, half * 12 + (tap - 1) * HALF + n + 1)
                                    dve.scalar_tensor_tensor(out=to, in0=src, scalar=cols[:, at:at + 1], in1=to,
                                                             op0=ALU.mult, op1=ALU.add).then_inc(conv_step, 1)

                    def y_rows(half, t):
                        dve.wait_ge(b_ps, 2 * half + t + 1)
                        dve.wait_ge(conv_step, 12 * (half + 1))
                        if half == 1:
                            dve.wait_ge(y_lo_done, t + 1)
                        dve.tensor_tensor(pair[:, t, :].rearrange("p (k n) -> p k n", k=HALF), tp4[t],
                                          conv_buf[:, half * HALF:(half + 1) * HALF, t * P:(t + 1) * P],
                                          ALU.mult).then_inc(y_f_ready, 1)

                    def y_lo_conv(half, t):
                        ks, ts = slice(half * HALF, (half + 1) * HALF), slice(t * P, (t + 1) * P)
                        dve.wait_ge(y_hi_done, 2 * half + t + 1)
                        dve.tensor_tensor(y_lo[:, ks, ts], pair[:, t, :].rearrange("p (k n) -> p k n", k=HALF),
                                          y_hi[:, ks, ts].bitcast(F32), ALU.subtract).then_inc(y_lo_done, 1)

                    def unit(q, pieces):
                        split_in(u + q, (u + q) % 2, pieces)

                    unit(1, (0, 1, 2, 3))
                    unit(2, (0, 1))
                    z_rows(0, 1, 0)
                    unit(2, (2, 3))
                    z_rows(0, 1, 1)
                    unit(3, (0, 1, 2, 3))
                    split_out(o, o % 2)
                    unit(4, (0, 1))
                    z_rows(1, 3, 0)
                    taps(0)
                    unit(4, (2, 3))
                    z_rows(1, 3, 1)
                    unit(5, (0, 1, 2, 3))
                    split_out(o + 1, (o + 1) % 2)
                    taps(1)
                    split_in(next_u, next_u % 2, (0, 1))
                    y_rows(0, 0)
                    y_lo_conv(0, 0)
                    y_rows(0, 1)
                    y_lo_conv(0, 1)
                    split_in(next_u, next_u % 2, (2, 3))
                    y_rows(1, 0)
                    y_rows(1, 1)
                    y_lo_conv(1, 0)
                    y_lo_conv(1, 1)
                    split_out(o + 2, (o + 2) % 2)
                    split_out(o + 3, (o + 3) % 2)
                else:
                    def rope_products(n):
                        unit, t = divmod(n, 2)
                        heads = NKV if unit == 0 else 8
                        dve.wait_ge(proj_done, 2 * (u + unit) + t + 1)
                        if n < 2:
                            dve.wait_ge(v_ready, n + 1)
                        if n >= 1:
                            dve.wait_ge(rope_out, rope_writes(n))
                        src = proj[t][:, 0:heads * HD].rearrange("p (h d) -> p h d", d=HD // 2)
                        for to, table in ((rope_cos, cos_t), (rope_sin, sin_t)):
                            both = dve.tensor_tensor(to[:, 0:heads * HD].rearrange("p (h d) -> p h d", d=HD // 2), src,
                                                     table[:, t, :].unsqueeze(1).to_broadcast([P, 2 * heads, HD // 2]),
                                                     ALU.mult)
                        both.then_inc(rope_ab, 1)

                    def mask_max(g):
                        t, heads = attention_group(g)
                        keys = W // len(heads)
                        dve.wait_ge(scores_done, g + 1)
                        if g >= 2:
                            dve.wait_ge(probT_ps, g - 1)
                        buf = pair[:, g % 2, :].rearrange("p (h n) -> p h n", n=keys)
                        dve.scalar_tensor_tensor(out=buf, in0=scores[g % 2][:, :].rearrange("p (h n) -> p h n", n=keys),
                                                 scalar=1.0 / math.sqrt(HD),
                                                 in1=band[:, 2 * P - keys:2 * P].unsqueeze(1).to_broadcast([P, len(heads), keys]),
                                                 op0=ALU.mult, op1=ALU.add).then_inc(masked, 1)
                        dve.wait_ge(masked, g + 1)
                        hs = slice(heads[0], heads[-1] + 1, 2)
                        dve.tensor_reduce(sink_arg[:, t, hs], buf, AX.X, ALU.max, negate=True).then_inc(max_step, 1)
                        dve.wait_ge(max_step, 2 * g + 1)
                        dve.tensor_tensor(neg_max[:, t, hs], sink_arg[:, t, hs], neg_sink[:, hs],
                                          ALU.min).then_inc(max_step, 1)
                        dve.wait_ge(max_step, 2 * g + 2)
                        dve.tensor_tensor(sink_arg[:, t, hs], neg_max[:, t, hs], neg_sink[:, hs],
                                          ALU.subtract).then_inc(neg_max_ready, 1)

                    def probs_out(g):
                        dve.wait_ge(probT_ps, g + 1)
                        if g >= 2:
                            dve.wait_ge(pv_done, g - 1)
                        dve.tensor_copy(pT[:, g % 2, :], pT_ps[:, :]).then_inc(probT_ready, 1)

                    def normalise(b):
                        half, t = divmod(b, 2)
                        hs = slice(8 * half, 8 * half + 8)
                        last = {v: k for k, v in BATCH_LAST.items()}[b]
                        dve.wait_ge(exp_done, exps_through(last))
                        dve.wait_ge(sink_exp_done, b + 1)
                        dve.tensor_tensor(denom[:, t, hs], prob_sum[:, t, hs], sink_exp[:, t, hs],
                                          ALU.add).then_inc(den_step, 1)
                        dve.wait_ge(den_step, 2 * b + 1)
                        dve.reciprocal(inv_denom[:, t, hs], denom[:, t, hs]).then_inc(den_step, 1)
                        dve.wait_ge(den_step, 2 * b + 2)
                        dve.wait_ge(pv_done, last + 1)
                        if b >= 2:
                            dve.wait_ge(o_ps_T, b - 1)
                        dve.tensor_tensor(o_tok[:, t, :].rearrange("p (h d) -> p h d", d=HD),
                                          o_ps[:, :].rearrange("p (h d) -> p h d", d=HD),
                                          inv_denom[:, t, hs].unsqueeze(2).to_broadcast([P, 8, HD]),
                                          ALU.mult).then_inc(o_ready, 1)

                    def y_lo_attn(b):
                        half, t = divmod(b, 2)
                        ks, ts = slice(half * HALF, (half + 1) * HALF), slice(t * P, (t + 1) * P)
                        dve.wait_ge(y_hi_done, 4 + b + 1)
                        dve.tensor_tensor(y_lo[:, ks, ts], tp4[t], y_hi[:, ks, ts].bitcast(F32),
                                          ALU.subtract).then_inc(y_lo_done, 1)

                    dve.wait_ge(trig_ready, 2)
                    for t in range(NT):
                        dve.wait_ge(rstd_ready, 2 * m + t + 1)
                        for table in (cos_t, sin_t):
                            dve.tensor_scalar(table[:, t, :], table[:, t, :], rstd_col[0][:, t:t + 1], None,
                                              ALU.mult).then_inc(tables_ready, 1)
                    split_in(u + 1, (u + 1) % 2, (0, 1))
                    dve.wait_ge(tables_ready, 4)
                    rope_products(0)
                    split_in(u + 1, (u + 1) % 2, (2, 3))
                    rope_products(1)
                    split_in(u + 2, (u + 2) % 2, (0, 1))
                    rope_products(2)
                    split_in(u + 2, (u + 2) % 2, (2, 3))
                    rope_products(3)
                    split_out(o, o % 2)
                    rope_products(4)
                    mask_max(0)
                    for g in range(GROUPS):
                        if g + 1 < GROUPS and g not in (5,):
                            mask_max(g + 1)
                        if g == 2:
                            rope_products(5)
                        if g == 6:
                            y_lo_attn(1)
                        probs_out(g)
                        if g in BATCH_LAST:
                            normalise(BATCH_LAST[g])
                        if g == 5:
                            mask_max(6)
                        if g in (3, 9):
                            y_lo_attn(0 if g == 3 else 2)
                        if g < 2:
                            split_out(o + 1, (o + 1) % 2, (g,))
                        elif g < 6:
                            split_in(next_u, next_u % 2, (g - 2,))
                    y_lo_attn(3)
                    split_out(o + 2, (o + 2) % 2)
                    split_out(o + 3, (o + 3) % 2)
                for t in range(NT):
                    residual(m + 1, t, 0.5 if kind == FF else 1.0)
                    if s + 1 < len(STAGES):
                        norm_lo(m + 1, t)
            i = 2 * len(STAGES)
            dve.wait_ge(g_fin_landed, 16)
            for t in range(NT):
                dve.wait_ge(rstd_ready, i + t + 1)
                dve.scalar_tensor_tensor(out=fin[:, t, :], in0=x[:, t, :], scalar=rstd[:, i + t:i + t + 1],
                                         in1=g_fin, op0=ALU.mult, op1=ALU.mult).then_inc(fin_ready, 1)

        @block.tensor
        def _(pe):
            def project(m, u, t, slot, ks=range(KD), first=False):
                if 0 in ks and not first:
                    pe.wait_ge(in_lo_done, PIECES * (u + 1))
                for k in ks:
                    if first and k % HALF == 0:
                        pe.wait_ge(xT_lo_done, 4 * m + 2 * t + k // HALF + 1)
                    if first and t == 0 and k % 2 == 0:
                        pe.wait_ge(in_lo_done, PIECES * u + k // 2 + 1)
                    x_hi, x_lo = (a[:, k, t * P:(t + 1) * P] for a in (xT_hi, xT_lo))
                    pe.matmul(proj[t][:, :], x_hi, in_hi[:, slot, k, :], start=(k == 0), stop=False)
                    pe.matmul(proj[t][:, :], x_hi, in_lo[:, slot, k, :], start=False, stop=False)
                    last = pe.matmul(proj[t][:, :], x_lo, in_hi[:, slot, k, :], start=False, stop=(k == KD - 1))
                if KD - 1 in ks:
                    last.then_inc(proj_done, 1)

            def down(hi, lo, t, slot, kt, start, stop):
                for a, w, n in ((hi, out_hi, 0), (hi, out_lo, 1), (lo, out_hi, 2)):
                    for half in range(2):
                        last = pe.matmul(acc[t][half][:, :], a, w[:, slot, kt, half * W:(half + 1) * W],
                                         start=(start and n == 0), stop=(stop and n == 2))
                return last

            def down_hidden(c, o, t, h_slot, slot, kts=(0, 1), start=False, stop=False):
                for kt in kts:
                    last = down(*(a[:, h_slot, kt, t * P:(t + 1) * P] for a in (hT_hi, hT_lo)), t, slot, kt,
                                start=(start and kt == 0), stop=(stop and kt == 1))
                return last

            def down_mixed(mix, n, o, t):
                pe.wait_ge(y_lo_done, 4 * mix + 2 * (n // 2) + t + 1)
                pe.wait_ge(out_lo_done, 2 * (o + n) + 2)
                for kt in range(2):
                    last = down(*(a[:, 2 * n + kt, t * P:(t + 1) * P] for a in (y_hi, y_lo)), t, (o + n) % 2, kt,
                                start=(n == 0 and kt == 0), stop=(n == 3 and kt == 1))
                return last

            def transpose_x(m, t):
                for half in range(2):
                    if m == 0:
                        pe.wait_ge(x_landed[t], 16)
                    else:
                        pe.wait_ge(x_ready, 4 * (m - 1) + 2 * t + half + 1)
                    if t == 1:
                        pe.wait_ge(gained, 4 * m + half + 1)
                    for n in range(HALF):
                        k = half * HALF + n
                        last = pe.transpose(tp[half][:, n * P:(n + 1) * P], x[:, t, k * P:(k + 1) * P], ident[:, :])
                    last.then_inc(xT_ps, 1)

            def transpose_hidden(c):
                pe.wait_ge(h_ready, 2 * c + 2)
                if not isinstance(c, int) or c >= 1:
                    pe.wait_ge(hT_lo_done, c)
                for kt in range(2):
                    for t in range(NT):
                        last = pe.transpose(tp[0][:, kt * SEQ + t * P:kt * SEQ + (t + 1) * P],
                                            hid_buf[:, t, kt * P:(kt + 1) * P], ident[:, :])
                last.then_inc(hT_ps, 1)

            def transpose_rows(rows_of, bank, done):
                for n in range(HALF):
                    last = pe.transpose(tp[bank][:, n * P:(n + 1) * P], rows_of[:, n * P:(n + 1) * P], ident[:, :])
                last.then_inc(done, 1)

            pe.wait_ge(ident_ready, 2)
            pe.wait_ge(rows_landed, 16 * (len(STAGES) + 1))
            n_rows = GAIN_ROWS + CONV_ROWS
            pe.transpose(tp[0][:, 0:n_rows], rows[:, :], ident[0:n_rows, 0:n_rows]).then_inc(cols_ps, 1)
            pe.wait_ge(cols_ready, 1)
            transpose_x(0, 0)

            for s, kind in enumerate(STAGES):
                u, o, m = IN_BASE[s], OUT_BASE[s], s
                last_stage = s + 1 == len(STAGES)
                project(m, u, 0, u % 2, range(0, HALF), first=True)
                transpose_x(m, 1)
                project(m, u, 0, u % 2, range(HALF, KD), first=True)
                project(m, u, 1, u % 2, first=True)
                if kind == FF:
                    c = NJ * FF_INDEX[s]

                    def middle(j, par, start=False):
                        for t in range(NT):
                            pe.wait_ge(h_ready, 2 * (c + j - 1) + t + 1)
                            project(m, u + j, t, (u + par) % 2)
                            if t == 0:
                                transpose_hidden(c + j - 1)
                        pe.wait_ge(hT_lo_done, c + j)
                        pe.wait_ge(out_lo_done, 2 * (o + j))
                        for t in range(NT):
                            last = down_hidden(c + j - 1, o + j - 1, t, (c + par + 1) % 2, (o + par + 1) % 2, start=start)
                        last.then_inc(out_used, 1)

                    middle(1, 1, start=True)
                    with pe.Fori(0, LOOP_TURNS) as i:
                        for b in range(2):
                            middle(LOOP_FROM + 2 * i + b, b)
                    j = NJ - 1
                    for t in range(NT):
                        pe.wait_ge(h_ready, 2 * (c + j - 1) + t + 1)
                        project(m, u + j, t, (u + j) % 2)
                        if t == 0:
                            transpose_hidden(c + j - 1)
                    pe.wait_ge(hT_lo_done, c + j)
                    pe.wait_ge(out_lo_done, 2 * (o + j))
                    before = (c + j - 1, o + j - 1)
                    slots = ((c + j - 1) % 2, (o + j - 1) % 2)
                    down_hidden(*before, 0, *slots, kts=(0,))
                    transpose_hidden(c + j)
                    down_hidden(*before, 0, *slots, kts=(1,))
                    pe.wait_ge(hT_lo_done, c + j + 1)
                    pe.wait_ge(out_lo_done, 2 * (o + j + 1))
                    down_hidden(c + j, o + j, 0, (c + j) % 2, (o + j) % 2, stop=True).then_inc(acc_first, 1)
                    down_hidden(*before, 1, *slots).then_inc(out_used, 1)
                    if not last_stage:
                        transpose_x(m + 1, 0)
                    down_hidden(c + j, o + j, 1, (c + j) % 2, (o + j) % 2, stop=True).then_inc(out_used, 1)
                elif kind == CONV:
                    def unit(q, t, *free):
                        for semaphore, count in free:
                            pe.wait_ge(semaphore, count)
                        project(m, u + q, t, (u + q) % 2)

                    def transpose_z(half, t):
                        pe.wait_ge(z_ready, 2 * half + t + 1)
                        if half == 1:
                            pe.wait_ge(z_feat_ready, t + 1)
                        transpose_rows(z_tok[:, t, :], t, z_ps)

                    def transpose_b(half, t):
                        pe.wait_ge(c_ready, 4 + 2 * half + t + 1)
                        if half == 0:
                            pe.wait_ge(z_feat_ready, 2 + t + 1)
                        else:
                            pe.wait_ge(y_f_ready, t + 1)
                        transpose_rows(c_tok[:, t, :], t, b_ps)

                    unit(1, 0, (c_ready, 1))
                    unit(1, 1, (c_ready, 2))
                    unit(2, 0, (z_ready, 1))
                    transpose_z(0, 0)
                    unit(2, 1, (z_ready, 2))
                    transpose_z(0, 1)
                    unit(3, 0, (c_ready, 3))
                    unit(3, 1, (c_ready, 4))
                    unit(4, 0, (z_ready, 3))
                    transpose_z(1, 0)
                    transpose_z(1, 1)
                    unit(4, 1, (z_ready, 4))
                    unit(5, 0, (c_ready, 5))
                    transpose_b(0, 0)
                    transpose_b(0, 1)
                    unit(5, 1, (c_ready, 6))
                else:
                    def queries(n, t, ks=range(KD)):
                        if 0 in ks:
                            pe.wait_ge(rope_ab, 2 * (n - 1) + t + 1)
                            if n == 1:
                                pe.wait_ge(v_ready, t + 1)
                        project(m, u + n, t, (u + n) % 2, ks)

                    def transpose_qk(n):
                        pe.wait_ge(rope_out, rope_writes(n + 1))
                        if n >= 2:
                            pe.wait_ge(qkT_ready, n - 1)
                        if n >= 4:
                            pe.wait_ge(y_lo_done, 4 + 1)
                        transpose_rows((kd_tok if n < 2 else q_tok)[:, n % 2, :], n % 2, qk_ps)

                    def score(g):
                        t, heads = attention_group(g)
                        keys = W // len(heads)
                        pe.wait_ge(qkT_ready, 4 if g < 6 else 6)
                        if g >= 2:
                            pe.wait_ge(masked, g - 1)
                        for n, h in enumerate(heads):
                            ps = slice(HD * (h % 2), HD * (h % 2) + HD)
                            last = pe.matmul(scores[g % 2][:, n * keys:(n + 1) * keys],
                                             qT[ps, h // 2, t * P:(t + 1) * P], kT[ps, h // 4, 0:keys],
                                             start=True, stop=True)
                        last.then_inc(scores_done, 1)

                    def transpose_probs(g):
                        pe.wait_ge(exp_done, exps_through(g))
                        if g >= 1:
                            pe.wait_ge(probT_ready, g)
                        for n in range(HALF):
                            last = pe.transpose(pT_ps[:, n * P:(n + 1) * P], pair[:, g % 2, n * P:(n + 1) * P], ident[:, :])
                        last.then_inc(probT_ps, 1)

                    def values(g):
                        t, heads = attention_group(g)
                        blocks = 1 + t
                        pe.wait_ge(probT_ready, g + 1)
                        if g in (2, 6, 8):
                            pe.wait_ge(o_ready, {2: 1, 6: 2, 8: 3}[g])
                        for n, h in enumerate(heads):
                            for b in range(blocks):
                                at = n * blocks + b
                                last = pe.matmul(o_ps[:, (h % 8) * HD:(h % 8 + 1) * HD],
                                                 pT[:, g % 2, at * P:(at + 1) * P],
                                                 v_tok[:, b, (h // 4) * HD:(h // 4 + 1) * HD],
                                                 start=(b == 0), stop=(b == blocks - 1))
                        last.then_inc(pv_done, 1)

                    def transpose_o(b):
                        pe.wait_ge(o_ready, b + 1)
                        if b >= 2:
                            pe.wait_ge(y_lo_done, 4 + b - 1)
                        if b < 2:
                            pe.wait_ge(qkT_ready, 4 if b == 0 else 6)
                        transpose_rows(o_tok[:, b % 2, :], b % 2, o_ps_T)

                    queries(1, 0)
                    transpose_qk(0)
                    transpose_qk(1)
                    queries(1, 1)
                    queries(2, 0, range(0, 5))
                    transpose_qk(2)
                    transpose_qk(3)
                    queries(2, 0, range(5, KD))
                    score(0)
                    score(1)
                    queries(2, 1, range(0, 2))
                    for g in range(GROUPS):
                        transpose_probs(g)
                        if g % 6 < 4:
                            score(g + 2)
                        if g < 3:
                            queries(2, 1, range(2 + 2 * g, 4 + 2 * g))
                        values(g)
                        if g == 2:
                            transpose_o(0)
                        if g == 5:
                            transpose_qk(4)
                            transpose_qk(5)
                            score(6)
                            score(7)
                            transpose_o(1)
                        if g == 8:
                            transpose_o(2)
                    transpose_o(3)
                if kind != FF:
                    mix = MIX_INDEX[s]
                    for n in range(2):
                        down_mixed(mix, n, o, 0)
                        if kind == CONV and n == 0:
                            transpose_b(1, 0)
                            transpose_b(1, 1)
                        down_mixed(mix, n, o, 1).then_inc(out_used, 1)
                    down_mixed(mix, 2, o, 0)
                    down_mixed(mix, 3, o, 0).then_inc(acc_first, 1)
                    down_mixed(mix, 2, o, 1).then_inc(out_used, 1)
                    transpose_x(m + 1, 0)
                    down_mixed(mix, 3, o, 1).then_inc(out_used, 1)


_INS = ["x", "positions", "ln_ff1", "w_ff1_in", "w_ff1_out", "ln_mix", "ln_ff2", "w_ff2_in", "w_ff2_out",
        "conv_w_in", "conv_kernel", "conv_w_out", "attn_w_qkv", "attn_sinks", "attn_w_o", "ln_final"]


def kernel(**inputs):
    import concourse.bacc as bacc
    from concourse.bass_utils import run_bass_kernel_spmd

    nc = bacc.Bacc("TRN2", target_bir_lowering=False, num_devices=1)
    arrays, args = {}, []
    freq = (THETA ** (-np.arange(0, HD, 2, dtype=np.float64) / HD)).astype(np.float32)
    given = {name: np.ascontiguousarray(inputs[name]) for name in _INS}
    given["inv_freq"] = np.ascontiguousarray(np.broadcast_to(freq, (P, HD // 2)))
    for name, a in given.items():
        arrays[f"in_{name}"] = a
        args.append(nc.dram_tensor(f"in_{name}", a.shape, mybir.dt.from_np(a.dtype), kind="ExternalInput").ap())
    args.append(nc.dram_tensor("out_0", (1, SEQ, D), F32, kind="ExternalOutput").ap())
    build(nc, *args)
    r = run_bass_kernel_spmd(nc, [arrays], core_ids=[0])
    return r.results[0]["out_0"]
```

```python
from contextlib import ExitStack
import math

import numpy as np

import concourse.bass as bass
from concourse import mybir

F32 = mybir.dt.float32
F32R = mybir.dt.float32r
I32 = mybir.dt.int32
ALU = mybir.AluOpType
ACT = mybir.ActivationFunctionType
AX = mybir.AxisListType

P = 128
D = 1024
SEQ = 256
NT = SEQ // P
KD = D // P
F = 2816
UNIT = 256
NJ = F // UNIT
W = 512
HALF = KD // 2
HD = 64
NKV = 4
NQ = 16
EPS = 1e-6
THETA = 10000.0
NEG = -3.4028234663852886e38

FF, CONV, ATTN = "ff", "conv", "attn"
STAGES = [FF, CONV, FF, FF, ATTN, FF]
IN_UNITS = {FF: NJ, CONV: 3 * D // W, ATTN: (NQ + 2 * NKV) * HD // W}
OUT_UNITS = {FF: NJ, CONV: D // UNIT, ATTN: D // UNIT}
IN_BASE = [sum(IN_UNITS[k] for k in STAGES[:s]) for s in range(len(STAGES) + 1)]
OUT_BASE = [sum(OUT_UNITS[k] for k in STAGES[:s]) for s in range(len(STAGES) + 1)]
FF_INDEX = {0: 0, 2: 1, 3: 2, 5: 3}
WARM_UP = 18
PIECES = 4
LOOP_FROM, LOOP_TURNS = 2, 4

CONV_COLS = [D, 2 * D, D + W, 2 * D + W, 0, W]
ATTN_COLS = [NQ * HD, 0, W]

GAIN_ROWS = len(STAGES) * KD
CONV_ROWS = 3 * KD


def two_pi_parts(count, bits):
    parts, rest = [], 2 * math.pi
    for _ in range(count - 1):
        _, e = math.frexp(rest)
        step = 2.0 ** (e - bits)
        part = math.floor(rest / step) * step
        parts.append(part)
        rest -= part
    return parts + [rest]


def attention_group(g):
    chunk, r = divmod(g, 6)
    if r < 2:
        return 0, list(range(8 * chunk + r, 8 * chunk + 8, 2))
    first = 8 * chunk + (0, 1, 4, 5)[r - 2]
    return 1, [first, first + 2]


GROUPS = 12
BATCH_LAST = [1, 5, 7, 11]


def exps_through(g):
    return sum(len(attention_group(n)[1]) for n in range(g + 1))


def late_out_at(n, kt):
    return 4 * (n - 2) + 2 * kt


def rope_writes(n):
    return 4 * n if n <= 2 else 8 + 2 * (n - 2)


def build(nc, x_in, positions, ln_ff1, w_ff1_in, w_ff1_out, ln_mix, ln_ff2, w_ff2_in, w_ff2_out,
          conv_w_in, conv_kernel, conv_w_out, attn_w_qkv, attn_sinks, attn_w_o, ln_final,
          inv_freq, out):
    w_in = {0: w_ff1_in[0], 1: conv_w_in[0], 2: w_ff2_in[0], 3: w_ff1_in[1], 4: attn_w_qkv[0], 5: w_ff2_in[1]}
    w_out = {0: w_ff1_out[0], 1: conv_w_out[0], 2: w_ff2_out[0], 3: w_ff1_out[1], 4: attn_w_o[0], 5: w_ff2_out[1]}
    gains = [ln_ff1, ln_mix, ln_ff2]

    with ExitStack() as ctx:
        def sb(name, shape, dt=F32):
            return ctx.enter_context(nc.sbuf_tensor(name, shape, dt))

        def sem(name):
            return ctx.enter_context(nc.semaphore(name))

        raw_in = sb("raw_in", [P, KD, W])
        raw_out = sb("raw_out", [P, 2, D])
        in_hi = sb("in_hi", [P, 2, KD, W], F32R)
        in_lo = sb("in_lo", [P, 2, KD, W], F32R)
        out_hi = sb("out_hi", [P, 2, 2, D], F32R)
        out_lo = sb("out_lo", [P, 2, 2, D], F32R)
        x = sb("x", [P, NT, D])
        xT_hi = sb("xT_hi", [P, KD, SEQ], F32R)
        xT_lo = sb("xT_lo", [P, KD, SEQ], F32R)
        hT_hi = sb("hT_hi", [P, 2, 2, SEQ], F32R)
        hT_lo = sb("hT_lo", [P, 2, 2, SEQ], F32R)
        y_hi = sb("y_hi", [P, KD, SEQ], F32R)
        y_lo = sb("y_lo", [P, KD, SEQ], F32R)
        pair = sb("pair", [P, 2, W])
        gated = sb("gated", [P, 2 * W])
        scratch = sb("scratch", [P, 6656])
        ident = sb("ident", [P, P])
        band = sb("band", [P, 2 * P])
        rows = sb("rows", [GAIN_ROWS + CONV_ROWS, P])
        cols = sb("cols", [P, GAIN_ROWS + CONV_ROWS])
        sink = sb("sink", [P, NQ])
        neg_sink = sb("neg_sink", [P, NQ])
        freq = sb("freq", [P, HD // 2])
        pos_i = sb("pos_i", [P, NT], I32)
        pos_f = sb("pos_f", [P, NT])
        angle = sb("angle", [P, NT, HD // 2])
        turns = sb("turns", [P, NT, HD // 2])
        sin_t = sb("sin_t", [P, NT, HD // 2])
        cos_t = sb("cos_t", [P, NT, HD // 2])
        sq_sum = sb("sq_sum", [P, 2 * 7])
        mean_sq = sb("mean_sq", [P, 2 * 7])
        rstd = sb("rstd", [P, 2 * 7])
        minus_half = sb("minus_half", [P, 1])
        warm = sb("warm", [P, 1])
        row_max = sb("row_max", [P, NT, NQ])
        neg_max = sb("neg_max", [P, NT, NQ])
        sink_arg = sb("sink_arg", [P, NT, NQ])
        sink_exp = sb("sink_exp", [P, NT, NQ])
        prob_sum = sb("prob_sum", [P, NT, NQ])
        denom = sb("denom", [P, NT, NQ])
        inv_denom = sb("inv_denom", [P, NT, NQ])

        silu_buf = gated[:, 0:W].rearrange("p (t n) -> p t n", t=NT)
        hid_buf = gated[:, W:2 * W].rearrange("p (t n) -> p t n", t=NT)
        rope_cos = gated[:, 0:W]
        rope_sin = gated[:, W:2 * W]

        c_tok = scratch[:, 0:1024].rearrange("p (t n) -> p t n", t=NT)
        z_tok = scratch[:, 1024:2048].rearrange("p (t n) -> p t n", t=NT)
        PAD = SEQ + 2
        z_feat = scratch[:, 2048:2048 + KD * PAD].rearrange("p (k n) -> p k n", k=KD)
        conv_at = 2048 + KD * PAD
        conv_buf = scratch[:, conv_at:conv_at + KD * SEQ].rearrange("p (k n) -> p k n", k=KD)
        q_tok = scratch[:, 0:1024].rearrange("p (t n) -> p t n", t=NT)
        kd_tok = scratch[:, 1024:2048].rearrange("p (t n) -> p t n", t=NT)
        o_tok = kd_tok
        v_tok = scratch[:, 2048:2560].rearrange("p (t n) -> p t n", t=NT)
        qT = scratch[:, 2560:4608].rearrange("p (h n) -> p h n", h=NQ // 2)
        kT = scratch[:, 4608:5632].rearrange("p (h n) -> p h n", h=NKV)
        pT = scratch[:, 5632:6656].rearrange("p (s n) -> p s n", s=2)
        g_fin = scratch[:, 0:D]
        fin = scratch[:, D:3 * D].rearrange("p (t n) -> p t n", t=NT)

        acc = [[ctx.enter_context(nc.psum_tensor(f"acc{t}{h}", [P, W], F32)) for h in range(2)] for t in range(NT)]
        proj = [ctx.enter_context(nc.psum_tensor(f"proj{t}", [P, W], F32)) for t in range(NT)]
        tp = [ctx.enter_context(nc.psum_tensor(f"tp{i}", [P, W], F32)) for i in range(2)]
        tp4 = [b[:, :].rearrange("p (k n) -> p k n", k=HALF) for b in tp]
        scores = [acc[0], proj]
        pT_ps = [acc[1][0], tp[0]]
        o_ps = [acc[1][1], tp[1]]
        oT_ps = [0, 1, 0, 0]

        x_landed = [sem(f"x_landed{t}") for t in range(NT)]
        rows_landed = sem("rows_landed")
        pos_landed = sem("pos_landed")
        g_fin_landed = sem("g_fin_landed")
        in_landed = [sem(f"in_landed{q}") for q in range(PIECES)]
        out_landed = [sem(f"out_landed{h}") for h in range(2)]
        in_hi_done = sem("in_hi_done")
        in_lo_done = sem("in_lo_done")
        out_hi_done = sem("out_hi_done")
        out_lo_done = sem("out_lo_done")
        proj_done = sem("proj_done")
        out_used = sem("out_used")
        acc_first = sem("acc_first")
        acc_half = sem("acc_half")
        x_ready = sem("x_ready")
        xT_ps = sem("xT_ps")
        gained = sem("gained")
        xT_hi_done = sem("xT_hi_done")
        xT_lo_done = sem("xT_lo_done")
        sq_ready = sem("sq_ready")
        mean_ready = sem("mean_ready")
        rstd_ready = sem("rstd_ready")
        silu_done = sem("silu_done")
        h_ready = sem("h_ready")
        hT_ps = sem("hT_ps")
        hT_hi_done = sem("hT_hi_done")
        hT_lo_done = sem("hT_lo_done")
        ident_ready = sem("ident_ready")
        consts_ready = sem("consts_ready")
        cols_ps = sem("cols_ps")
        cols_ready = sem("cols_ready")
        vec_step = sem("vec_step")
        trig_arg = sem("trig_arg")
        trig_ready = sem("trig_ready")
        pads_ready = sem("pads_ready")
        c_ready = sem("c_ready")
        z_ready = sem("z_ready")
        z_ps = sem("z_ps")
        z_feat_ready = sem("z_feat_ready")
        conv_step = sem("conv_step")
        b_ps = sem("b_ps")
        y_f_ready = sem("y_f_ready")
        y_hi_done = sem("y_hi_done")
        y_lo_done = sem("y_lo_done")
        tables_ready = sem("tables_ready")
        v_ready = sem("v_ready")
        rope_ab = sem("rope_ab")
        rope_out = sem("rope_out")
        qk_ps = sem("qk_ps")
        qkT_ready = sem("qkT_ready")
        scores_done = sem("scores_done")
        masked = sem("masked")
        max_step = sem("max_step")
        neg_max_ready = sem("neg_max_ready")
        exp_done = sem("exp_done")
        sink_arg_ready = sem("sink_arg_ready")
        sink_exp_done = sem("sink_exp_done")
        probT_ps = sem("probT_ps")
        probT_ready = sem("probT_ready")
        pv_done = sem("pv_done")
        den_step = sem("den_step")
        o_ready = sem("o_ready")
        o_ps_T = sem("o_ps_T")
        fin_ready = sem("fin_ready")
        stored = sem("stored")

        def gain_of(m, half):
            layer, which = divmod(m, 3)
            at = (2 * which + layer) * KD + half * HALF
            return cols[:, at:at + HALF].unsqueeze(2).to_broadcast([P, HALF, P])

        block = ctx.enter_context(nc.Block())

        @block.sync
        def _(sp):
            def load_in(u, s, col, up=None, pieces=range(PIECES)):
                src = w_in[s].rearrange("(k p) n -> p k n", p=P)
                for q in pieces:
                    if not isinstance(u, int) or u >= 1:
                        sp.wait_ge(in_lo_done, PIECES * (u - 1) + q + 1)
                    ks = slice(2 * q, 2 * q + 2)
                    if up is None:
                        sp.dma_start(raw_in[:, ks, :], src[:, ks, bass.ds(col, W)]).then_inc(in_landed[q], 32)
                    else:
                        for n, at in enumerate((col, up)):
                            sp.dma_start(raw_in[:, ks, n * UNIT:(n + 1) * UNIT],
                                         src[:, ks, bass.ds(at, UNIT)]).then_inc(in_landed[q], 16)

            def load_out(o, s, row):
                for h in range(2):
                    if not isinstance(o, int) or o >= 1:
                        sp.wait_ge(out_lo_done, 2 * (o - 1) + h + 1)
                    sp.dma_start(raw_out[:, h, :], w_out[s][bass.ds(row + h * P, P), :]).then_inc(out_landed[h], 16)

            def first_in(s):
                if s == len(STAGES):
                    return
                col = {FF: 0, CONV: CONV_COLS[0], ATTN: ATTN_COLS[0]}[STAGES[s]]
                load_in(IN_BASE[s], s, col, F if STAGES[s] == FF else None)

            sp.dma_start(x[:, 0, :], x_in[0, 0:P, :]).then_inc(x_landed[0], 16)
            load_in(0, 0, 0, F, (0, 1))
            sp.dma_start(x[:, 1, :], x_in[0, P:2 * P, :]).then_inc(x_landed[1], 16)
            load_in(0, 0, 0, F, (2, 3))
            load_in(1, 0, UNIT, F + UNIT)
            sp.dma_start(sink[:, :], attn_sinks[0].partition_broadcast(P)).then_inc(pos_landed, 16)
            sp.dma_start(freq[:, :], inv_freq).then_inc(pos_landed, 16)
            with nc.allow_non_contiguous_dma(reason="256 positions, four bytes each"):
                sp.dma_start(pos_i[:, :], positions[0].rearrange("(t p) -> p t", p=P)).then_inc(pos_landed, 16)

            for s, kind in enumerate(STAGES):
                u, o = IN_BASE[s], OUT_BASE[s]
                if kind == FF:
                    if s > 0:
                        load_in(u + 1, s, UNIT, F + UNIT)
                    load_out(o, s, 0)
                    with sp.Fori(1, NJ - 1) as j:
                        load_in(u + 1 + j, s, (j + 1) * UNIT, (j + 1) * UNIT + F)
                        load_out(o + j, s, j * UNIT)
                    first_in(s + 1)
                    load_out(o + NJ - 1, s, (NJ - 1) * UNIT)
                elif kind == CONV:
                    for q in (1, 2, "out0", 3, "out1", 4, 5):
                        if isinstance(q, int):
                            load_in(u + q, s, CONV_COLS[q])
                        else:
                            load_out(o + int(q[3:]), s, int(q[3:]) * UNIT)
                    first_in(s + 1)
                    load_out(o + 2, s, 2 * UNIT)
                    load_out(o + 3, s, 3 * UNIT)
                else:
                    for q in (1, 2):
                        load_in(u + q, s, ATTN_COLS[q])
                    load_out(o, s, 0)
                    load_out(o + 1, s, UNIT)
                    first_in(s + 1)
                    load_out(o + 2, s, 2 * UNIT)
                    load_out(o + 3, s, 3 * UNIT)
                    sp.wait_ge(out_used, OUT_BASE[s + 1])
                    sp.dma_start(g_fin, ln_final.partition_broadcast(P)).then_inc(g_fin_landed, 16)
            sp.wait_ge(fin_ready, 2)
            sp.dma_start(out[0, 0:P, :], fin[:, 0, :]).then_inc(stored, 16)
            for half in range(2):
                part = slice(half * W, (half + 1) * W)
                sp.wait_ge(fin_ready, 2 + half + 1)
                sp.dma_start(out[0, P:2 * P, part], fin[:, 1, part]).then_inc(stored, 16)
            sp.wait_ge(stored, 16 * (NT + 1))

        @block.gpsimd
        def _(pool):
            pool.memset(ident[:, :], 0.0).then_inc(ident_ready, 1)
            pool.wait_ge(ident_ready, 1)
            pool.affine_select(out=ident[:, :], in_=ident[:, :], compare_op=ALU.not_equal, fill=1.0, base=0,
                               pattern=[[-1, P]], channel_multiplier=1).then_inc(ident_ready, 1)
            pool.memset(minus_half[:, :], -0.5).then_inc(consts_ready, 1)
            pool.memset(band[:, :], 0.0).then_inc(consts_ready, 1)
            pool.wait_ge(consts_ready, 2)
            pool.affine_select(out=band[:, :], in_=band[:, :], compare_op=ALU.is_ge, fill=NEG, base=-1,
                               pattern=[[1, 2 * P]], channel_multiplier=-1).then_inc(consts_ready, 1)
            pool.wait_ge(consts_ready, 3)
            pool.affine_select(out=band[:, :], in_=band[:, :], compare_op=ALU.is_ge, fill=NEG, base=P,
                               pattern=[[-1, 2 * P]], channel_multiplier=1).then_inc(consts_ready, 1)
            pool.memset(z_feat[:, :, 0:2], 0.0).then_inc(pads_ready, 1)

            def rope_sums(n):
                heads = NKV if n < 2 else 8
                a = rope_cos[:, 0:heads * HD].rearrange("p (h e d) -> p h e d", h=heads, e=2)
                b = rope_sin[:, 0:heads * HD].rearrange("p (h e d) -> p h e d", h=heads, e=2)
                pool.wait_ge(rope_ab, n + 1)
                if n >= 4:
                    pool.wait_ge(qk_ps, n - 1)
                if n < 2:
                    dst = kd_tok[:, n, :].rearrange("p (h c e d) -> p c h e d", h=heads, c=2, e=2)
                    dsts = [dst[:, 0], dst[:, 1]]
                else:
                    dsts = [q_tok[:, n % 2, :].rearrange("p (h e d) -> p h e d", h=heads, e=2)]
                for to in dsts:
                    pool.tensor_tensor(to[:, :, 0, :], a[:, :, 0, :], b[:, :, 1, :], ALU.subtract).then_inc(rope_out, 1)
                    pool.tensor_tensor(to[:, :, 1, :], a[:, :, 1, :], b[:, :, 0, :], ALU.add).then_inc(rope_out, 1)

            for m in range(len(STAGES) + 1):
                for t in range(NT):
                    i = 2 * m + t
                    pool.wait_ge(sq_ready, i + 1)
                    pool.tensor_scalar(mean_sq[:, i:i + 1], sq_sum[:, i:i + 1], 1.0 / D, EPS,
                                       ALU.mult, ALU.add).then_inc(mean_ready, 1)
                    pool.wait_ge(mean_ready, i + 1)
                    pool.tensor_tensor(rstd[:, i:i + 1], mean_sq[:, i:i + 1], minus_half[:, :],
                                       ALU.pow).then_inc(rstd_ready, 1)
                if m < len(STAGES) and STAGES[m] == ATTN:
                    for n in range(6):
                        rope_sums(n)

        @block.scalar
        def _(act):
            def split_in(u, slot, pieces):
                for q in pieces:
                    act.wait_ge(in_landed[q], 32 * (u + 1))
                    if q == 0 and (not isinstance(u, int) or u >= 2):
                        act.wait_ge(proj_done, 2 * (u - 1))
                    act.activation(in_hi[:, slot, 2 * q:2 * q + 2, :], raw_in[:, 2 * q:2 * q + 2, :],
                                   ACT.Copy).then_inc(in_hi_done, 1)

            def split_out(o, slot, halves=(0, 1)):
                for h in halves:
                    act.wait_ge(out_landed[h], 16 * (o + 1))
                    if h == 0 and (not isinstance(o, int) or o >= 2):
                        act.wait_ge(out_used, o - 1)
                    act.activation(out_hi[:, slot, h, :], raw_out[:, h, :], ACT.Copy).then_inc(out_hi_done, 1)

            def split_late_out(s, n, halves=(0, 1)):
                slot = (IN_BASE[s + 1] - 1) % 2
                for h in halves:
                    act.wait_ge(out_landed[h], 16 * (OUT_BASE[s] + n + 1))
                    if h == 0:
                        act.wait_ge(proj_done, 2 * IN_BASE[s + 1])
                    k = late_out_at(n, h)
                    act.activation(in_hi[:, slot, k:k + 2, :],
                                   raw_out[:, h, :].rearrange("p (k n) -> p k n", k=2), ACT.Copy).then_inc(out_hi_done, 1)

            def norm_hi(m, t):
                for half in range(2):
                    act.wait_ge(gained, 4 * m + 2 * t + half + 1)
                    act.activation(xT_hi[:, half * HALF:(half + 1) * HALF, t * P:(t + 1) * P],
                                   pair[:, half, :].rearrange("p (k n) -> p k n", k=HALF),
                                   ACT.Copy).then_inc(xT_hi_done, 1)

            def squares(m, t):
                if m == 0:
                    act.wait_ge(x_landed[t], 16)
                else:
                    act.wait_ge(x_ready, 4 * (m - 1) + 2 * t + 2)
                i = 2 * m + t
                if i >= 1:
                    act.wait_ge(sq_ready, i)
                act.activation(gated[:, :], x[:, t, :], ACT.Square, accum_out=sq_sum[:, i:i + 1]).then_inc(sq_ready, 1)

            def silu(c, u, t, first_of=None):
                act.wait_ge(proj_done, 2 * u + t + 1)
                if first_of is not None:
                    act.wait_ge(rstd_ready, 2 * first_of + t + 1)
                    act.wait_ge(sq_ready, 2 * first_of + 2)
                act.activation(silu_buf[:, t, :], proj[t][:, 0:UNIT], ACT.Silu,
                               scale=rstd_col[0][:, t:t + 1]).then_inc(silu_done, 1)

            def hidden_hi(c, slot):
                act.wait_ge(hT_ps, c + 1)
                act.activation(hT_hi[:, slot, :, :].rearrange("p k n -> p (k n)"), tp[0][:, :],
                               ACT.Copy).then_inc(hT_hi_done, 1)

            for n, g in enumerate(gains):
                act.dma_start(rows[n * 2 * KD:(n + 1) * 2 * KD, :],
                              g.rearrange("l (k p) -> (l k) p", p=P)).then_inc(rows_landed, 16)
            act.dma_start(rows[GAIN_ROWS:GAIN_ROWS + CONV_ROWS, :],
                          conv_kernel[0].rearrange("w (k p) -> (w k) p", p=P)).then_inc(rows_landed, 16)
            rstd_col = [None]
            split_in(0, 0, (0,))
            norm_hi(0, 0)
            split_in(0, 0, (1, 2, 3))
            norm_hi(0, 1)
            squares(0, 0)
            squares(0, 1)

            for s, kind in enumerate(STAGES):
                u, o, m = IN_BASE[s], OUT_BASE[s], s
                rstd_col[0] = rstd[:, 2 * m:2 * m + 2]
                next_u = IN_BASE[s + 1] if s + 1 < len(STAGES) else None
                if kind == FF:
                    c = NJ * FF_INDEX[s]
                    if s > 0 and STAGES[s - 1] != FF:
                        act.wait_ge(out_used, o)
                    split_in(u + 1, (u + 1) % 2, (0, 1))
                    silu(c, u, 0, m)
                    split_in(u + 1, (u + 1) % 2, (2, 3))
                    silu(c, u, 1, m)
                    split_out(o, o % 2)
                    if s == 0:
                        act.wait_ge(trig_arg, 1)
                        act.activation(sin_t[:, :, :], angle[:, :, :], ACT.Sin).then_inc(trig_ready, 1)
                        act.activation(cos_t[:, :, :], turns[:, :, :], ACT.Sin).then_inc(trig_ready, 1)

                    def middle(j, par):
                        silu(c + j, u + j, 0)
                        hidden_hi(c + j - 1, (c + par + 1) % 2)
                        split_in(u + j + 1, (u + par + 1) % 2, (0, 1, 2))
                        silu(c + j, u + j, 1)
                        split_in(u + j + 1, (u + par + 1) % 2, (3,))
                        split_out(o + j, (o + par) % 2)

                    middle(1, 1)
                    with act.Fori(0, LOOP_TURNS) as i:
                        for b in range(2):
                            middle(LOOP_FROM + 2 * i + b, b)
                    j = NJ - 1
                    silu(c + j, u + j, 0)
                    hidden_hi(c + j - 1, (c + j - 1) % 2)
                    split_out(o + j, (o + j) % 2)
                    if next_u:
                        split_in(next_u, next_u % 2, (0,))
                    silu(c + j, u + j, 1)
                    hidden_hi(c + j, (c + j) % 2)
                    if next_u:
                        split_in(next_u, next_u % 2, (1, 2, 3))
                elif kind == CONV:
                    def c_rows(n, q, t):
                        act.wait_ge(proj_done, 2 * (u + q) + t + 1)
                        if n == 0:
                            act.wait_ge(rstd_ready, 2 * m + t + 1)
                        if 1 <= n <= 2:
                            act.wait_ge(z_ready, 2 * (n - 1) + t + 1)
                        if n == 3:
                            act.wait_ge(b_ps, t + 1)
                        act.activation(c_tok[:, t, :], proj[t][:, :], ACT.Copy,
                                       scale=rstd_col[0][:, t:t + 1]).then_inc(c_ready, 1)

                    def z_to_features(half, t):
                        act.wait_ge(z_ps, 2 * half + t + 1)
                        act.activation(z_feat[:, half * HALF:(half + 1) * HALF, 2 + t * P:2 + (t + 1) * P],
                                       tp4[t], ACT.Copy).then_inc(z_feat_ready, 1)

                    def y_hi_conv(half, t):
                        act.wait_ge(y_f_ready, 2 * half + t + 1)
                        act.activation(y_hi[:, half * HALF:(half + 1) * HALF, t * P:(t + 1) * P],
                                       pair[:, t, :].rearrange("p (k n) -> p k n", k=HALF),
                                       ACT.Copy).then_inc(y_hi_done, 1)

                    def unit(q, pieces):
                        split_in(u + q, (u + q) % 2, pieces)

                    everything = range(PIECES)
                    unit(1, everything)
                    c_rows(0, 0, 0)
                    c_rows(0, 0, 1)
                    unit(2, everything)
                    split_out(o, o % 2)
                    unit(3, everything)
                    c_rows(1, 2, 0)
                    z_to_features(0, 0)
                    z_to_features(0, 1)
                    c_rows(1, 2, 1)
                    split_out(o + 1, (o + 1) % 2)
                    unit(4, everything)
                    unit(5, everything)
                    c_rows(2, 4, 0)
                    z_to_features(1, 0)
                    z_to_features(1, 1)
                    c_rows(2, 4, 1)
                    split_in(next_u, next_u % 2, (0, 1))
                    c_rows(3, 5, 0)
                    y_hi_conv(0, 0)
                    y_hi_conv(0, 1)
                    split_in(next_u, next_u % 2, (2, 3))
                    c_rows(3, 5, 1)
                    y_hi_conv(1, 0)
                    y_hi_conv(1, 1)
                    split_late_out(s, 2)
                    split_late_out(s, 3)
                else:
                    def v_rows(t):
                        act.wait_ge(proj_done, 2 * u + t + 1)
                        act.wait_ge(rstd_ready, 2 * m + t + 1)
                        act.activation(v_tok[:, t, :], proj[t][:, 256:512], ACT.Copy,
                                       scale=rstd_col[0][:, t:t + 1]).then_inc(v_ready, 1)

                    def qk_out(n):
                        act.wait_ge(qk_ps, n + 1)
                        t = n % 2
                        to = kT[:, :, t * P:(t + 1) * P] if n < 2 else \
                            qT[:, HALF * (n // 2 - 1):HALF * (n // 2), t * P:(t + 1) * P]
                        act.activation(to, tp4[t], ACT.Copy).then_inc(qkT_ready, 1)

                    def exps(g):
                        t, heads = attention_group(g)
                        act.wait_ge(neg_max_ready, g + 1)
                        keys = W // len(heads)
                        for n, h in enumerate(heads):
                            part = pair[:, g % 2, n * keys:(n + 1) * keys]
                            act.activation(part, part, ACT.Exp, bias=neg_max[:, t, h:h + 1],
                                           accum_out=prob_sum[:, t, h:h + 1]).then_inc(exp_done, 1)

                    def sink_exps(b):
                        half, t = divmod(b, 2)
                        hs = slice(8 * half, 8 * half + 8)
                        act.wait_ge(sink_arg_ready, b + 1)
                        act.activation(sink_exp[:, t, hs], sink_arg[:, t, hs], ACT.Exp).then_inc(sink_exp_done, 1)

                    def probs_out(g):
                        act.wait_ge(probT_ps, g + 1)
                        if g >= 2:
                            act.wait_ge(pv_done, g - 1)
                        act.activation(pT[:, g % 2, :], pT_ps[g // 6][:, :], ACT.Copy).then_inc(probT_ready, 1)

                    def y_hi_attn(b):
                        act.wait_ge(o_ps_T, b + 1)
                        half, t = divmod(b, 2)
                        act.activation(y_hi[:, half * HALF:(half + 1) * HALF, t * P:(t + 1) * P],
                                       tp4[oT_ps[b]], ACT.Copy).then_inc(y_hi_done, 1)

                    def next_piece(q):
                        split_in(next_u, next_u % 2, (q,))

                    split_in(u + 1, (u + 1) % 2, (0, 1))
                    v_rows(0)
                    split_in(u + 1, (u + 1) % 2, (2, 3))
                    v_rows(1)
                    split_in(u + 2, (u + 2) % 2, range(PIECES))
                    qk_out(0)
                    qk_out(1)
                    split_out(o, o % 2)
                    qk_out(2)
                    act.activation(warm[:, :], minus_half[:, :], ACT.Exp)
                    qk_out(3)
                    exps(0)
                    split_out(o + 1, (o + 1) % 2, (0,))
                    exps(1)
                    sink_exps(0)
                    probs_out(0)
                    split_out(o + 1, (o + 1) % 2, (1,))
                    exps(2)
                    probs_out(1)
                    next_piece(0)
                    exps(3)
                    probs_out(2)
                    exps(4)
                    y_hi_attn(0)
                    probs_out(3)
                    next_piece(1)
                    probs_out(4)
                    exps(5)
                    sink_exps(1)
                    next_piece(2)
                    qk_out(4)
                    probs_out(5)
                    exps(6)
                    qk_out(5)
                    probs_out(6)
                    y_hi_attn(1)
                    exps(7)
                    sink_exps(2)
                    next_piece(3)
                    exps(8)
                    probs_out(7)
                    split_late_out(s, 2, (0,))
                    exps(9)
                    probs_out(8)
                    y_hi_attn(2)
                    split_late_out(s, 2, (1,))
                    probs_out(9)
                    exps(10)
                    split_late_out(s, 3, (0,))
                    probs_out(10)
                    exps(11)
                    sink_exps(3)
                    split_late_out(s, 3, (1,))
                    probs_out(11)
                    y_hi_attn(3)
                for t in range(NT):
                    if s + 1 < len(STAGES):
                        norm_hi(m + 1, t)
                    squares(m + 1, t)

        @block.vector
        def _(dve):
            steps = [0]

            def step(instruction):
                instruction.then_inc(vec_step, 1)
                steps[0] += 1
                dve.wait_ge(vec_step, steps[0])

            def split_in(u, slot, pieces):
                for q in pieces:
                    dve.wait_ge(in_hi_done, PIECES * u + q + 1)
                    dve.tensor_tensor(in_lo[:, slot, 2 * q:2 * q + 2, :], raw_in[:, 2 * q:2 * q + 2, :],
                                      in_hi[:, slot, 2 * q:2 * q + 2, :].bitcast(F32),
                                      ALU.subtract).then_inc(in_lo_done, 1)

            def split_out(o, slot, halves=(0, 1)):
                for h in halves:
                    dve.wait_ge(out_hi_done, 2 * o + h + 1)
                    dve.tensor_tensor(out_lo[:, slot, h, :], raw_out[:, h, :], out_hi[:, slot, h, :].bitcast(F32),
                                      ALU.subtract).then_inc(out_lo_done, 1)

            def split_late_out(s, n, halves=(0, 1)):
                slot = (IN_BASE[s + 1] - 1) % 2
                for h in halves:
                    dve.wait_ge(out_hi_done, 2 * (OUT_BASE[s] + n) + h + 1)
                    k = late_out_at(n, h)
                    dve.tensor_tensor(in_lo[:, slot, k:k + 2, :],
                                      raw_out[:, h, :].rearrange("p (k n) -> p k n", k=2),
                                      in_hi[:, slot, k:k + 2, :].bitcast(F32),
                                      ALU.subtract).then_inc(out_lo_done, 1)

            def residual(m, t, scale):
                for half in range(2):
                    if t == 0:
                        dve.wait_ge(acc_first, m)
                    elif half == 0 and STAGES[m - 1] == FF:
                        dve.wait_ge(acc_half, FF_INDEX[m - 1] + 1)
                    else:
                        dve.wait_ge(out_used, OUT_BASE[m])
                    part = x[:, t, half * W:(half + 1) * W]
                    dve.scalar_tensor_tensor(out=part, in0=acc[t][half][:, :], scalar=scale, in1=part,
                                             op0=ALU.mult, op1=ALU.add).then_inc(x_ready, 1)

            def norm_lo(m, t):
                norm_gain(m, t)
                norm_rest(m, t)

            def norm_gain(m, t):
                for half in range(2):
                    n = 4 * m + 2 * t + half
                    dve.wait_ge(xT_ps, n + 1)
                    if n >= 2:
                        dve.wait_ge(xT_lo_done, n - 1)
                    dve.tensor_tensor(pair[:, half, :].rearrange("p (k n) -> p k n", k=HALF), tp4[half],
                                      gain_of(m, half), ALU.mult).then_inc(gained, 1)

            def norm_rest(m, t):
                for half in range(2):
                    n = 4 * m + 2 * t + half
                    ks, ts = slice(half * HALF, (half + 1) * HALF), slice(t * P, (t + 1) * P)
                    dve.wait_ge(xT_hi_done, n + 1)
                    dve.tensor_tensor(xT_lo[:, ks, ts], pair[:, half, :].rearrange("p (k n) -> p k n", k=HALF),
                                      xT_hi[:, ks, ts].bitcast(F32), ALU.subtract).then_inc(xT_lo_done, 1)

            def hidden(c, t):
                dve.wait_ge(silu_done, 2 * c + t + 1)
                if not isinstance(c, int) or c >= 1:
                    dve.wait_ge(hT_ps, c)
                dve.scalar_tensor_tensor(out=hid_buf[:, t, :], in0=proj[t][:, UNIT:2 * UNIT],
                                         scalar=rstd_col[0][:, t:t + 1], in1=silu_buf[:, t, :],
                                         op0=ALU.mult, op1=ALU.mult).then_inc(h_ready, 1)

            def hidden_lo(c, slot):
                dve.wait_ge(hT_hi_done, c + 1)
                dve.tensor_tensor(hT_lo[:, slot, :, :].rearrange("p k n -> p (k n)"), tp[0][:, :],
                                  hT_hi[:, slot, :, :].rearrange("p k n -> p (k n)").bitcast(F32),
                                  ALU.subtract).then_inc(hT_lo_done, 1)

            def rope_angles():
                dve.wait_ge(pos_landed, 48)
                step(dve.tensor_copy(pos_f[:, :], pos_i[:, :]))
                for t in range(NT):
                    step(dve.tensor_scalar(angle[:, t, :], freq[:, :], pos_f[:, t:t + 1], None, ALU.mult))
                magic = 1.5 * 2.0 ** 23
                step(dve.tensor_scalar(turns[:, :, :], angle[:, :, :], 1.0 / (2 * math.pi), magic, ALU.mult, ALU.add))
                step(dve.tensor_scalar(turns[:, :, :], turns[:, :, :], -magic, None, ALU.add))
                for part in two_pi_parts(4, 8):
                    step(dve.scalar_tensor_tensor(out=angle[:, :, :], in0=turns[:, :, :], scalar=-part,
                                                  in1=angle[:, :, :], op0=ALU.mult, op1=ALU.add))
                top = 3.1415925
                step(dve.tensor_scalar(angle[:, :, :], angle[:, :, :], top, -top, ALU.min, ALU.max))
                step(dve.scalar_tensor_tensor(out=turns[:, :, :], in0=angle[:, :, :], scalar=-1.0,
                                              in1=angle[:, :, :], op0=ALU.mult, op1=ALU.max))
                dve.tensor_scalar(turns[:, :, :], turns[:, :, :], -1.0, math.pi / 2, ALU.mult, ALU.add).then_inc(trig_arg, 1)
                dve.tensor_scalar(neg_sink[:, :], sink[:, :], -1.0, None, ALU.mult).then_inc(vec_step, 1)
                steps[0] += 1

            rstd_col = [None]
            dve.wait_ge(cols_ps, 1)
            dve.tensor_copy(cols[:, :], proj[1][:, 0:GAIN_ROWS + CONV_ROWS]).then_inc(cols_ready, 1)
            dve.wait_ge(cols_ready, 1)
            norm_gain(0, 0)
            split_in(0, 0, (0,))
            norm_rest(0, 0)
            split_in(0, 0, (1, 2, 3))
            norm_lo(0, 1)

            for s, kind in enumerate(STAGES):
                u, o, m = IN_BASE[s], OUT_BASE[s], s
                rstd_col[0] = rstd[:, 2 * m:2 * m + 2]
                next_u = IN_BASE[s + 1] if s + 1 < len(STAGES) else None
                if kind == FF:
                    c = NJ * FF_INDEX[s]
                    split_in(u + 1, (u + 1) % 2, (0, 1))
                    hidden(c, 0)
                    split_in(u + 1, (u + 1) % 2, (2, 3))
                    hidden(c, 1)
                    split_out(o, o % 2)
                    if s == 0:
                        rope_angles()

                    def middle(j, par):
                        hidden(c + j, 0)
                        hidden_lo(c + j - 1, (c + par + 1) % 2)
                        split_in(u + j + 1, (u + par + 1) % 2, (0, 1, 2))
                        hidden(c + j, 1)
                        split_in(u + j + 1, (u + par + 1) % 2, (3,))
                        split_out(o + j, (o + par) % 2)

                    middle(1, 1)
                    with dve.Fori(0, LOOP_TURNS) as i:
                        for b in range(2):
                            middle(LOOP_FROM + 2 * i + b, b)
                    j = NJ - 1
                    hidden(c + j, 0)
                    hidden_lo(c + j - 1, (c + j - 1) % 2)
                    split_out(o + j, (o + j) % 2)
                    if next_u:
                        split_in(next_u, next_u % 2, (0,))
                    hidden(c + j, 1)
                    hidden_lo(c + j, (c + j) % 2)
                    if next_u:
                        split_in(next_u, next_u % 2, (1, 2, 3))
                elif kind == CONV:
                    def z_rows(half, q, t):
                        dve.wait_ge(proj_done, 2 * (u + q) + t + 1)
                        dve.wait_ge(c_ready, 2 * half + t + 1)
                        if half == 1:
                            dve.wait_ge(z_ps, t + 1)
                        dve.scalar_tensor_tensor(out=z_tok[:, t, :], in0=proj[t][:, :],
                                                 scalar=rstd_col[0][:, t:t + 1], in1=c_tok[:, t, :],
                                                 op0=ALU.mult, op1=ALU.mult).then_inc(z_ready, 1)

                    def taps(half):
                        dve.wait_ge(z_feat_ready, 2 * half + 2)
                        dve.wait_ge(pads_ready, 1)
                        for tap in range(3):
                            for n in range(HALF):
                                k = half * HALF + n
                                at = GAIN_ROWS + tap * KD + k
                                src, to = z_feat[:, k, tap:tap + SEQ], conv_buf[:, k, :]
                                if tap == 0:
                                    dve.tensor_scalar(to, src, cols[:, at:at + 1], None,
                                                      ALU.mult).then_inc(conv_step, 1)
                                else:
                                    dve.wait_ge(conv_step, half * 12 + (tap - 1) * HALF + n + 1)
                                    dve.scalar_tensor_tensor(out=to, in0=src, scalar=cols[:, at:at + 1], in1=to,
                                                             op0=ALU.mult, op1=ALU.add).then_inc(conv_step, 1)

                    def y_rows(half, t):
                        dve.wait_ge(b_ps, 2 * half + t + 1)
                        dve.wait_ge(conv_step, 12 * (half + 1))
                        if half == 1:
                            dve.wait_ge(y_lo_done, t + 1)
                        dve.tensor_tensor(pair[:, t, :].rearrange("p (k n) -> p k n", k=HALF), tp4[t],
                                          conv_buf[:, half * HALF:(half + 1) * HALF, t * P:(t + 1) * P],
                                          ALU.mult).then_inc(y_f_ready, 1)

                    def y_lo_conv(half, t):
                        ks, ts = slice(half * HALF, (half + 1) * HALF), slice(t * P, (t + 1) * P)
                        dve.wait_ge(y_hi_done, 2 * half + t + 1)
                        dve.tensor_tensor(y_lo[:, ks, ts], pair[:, t, :].rearrange("p (k n) -> p k n", k=HALF),
                                          y_hi[:, ks, ts].bitcast(F32), ALU.subtract).then_inc(y_lo_done, 1)

                    def unit(q, pieces):
                        split_in(u + q, (u + q) % 2, pieces)

                    everything = range(PIECES)
                    unit(1, everything)
                    unit(2, everything)
                    z_rows(0, 1, 0)
                    z_rows(0, 1, 1)
                    split_out(o, o % 2)
                    unit(3, everything)
                    taps(0)
                    split_out(o + 1, (o + 1) % 2)
                    unit(4, everything)
                    z_rows(1, 3, 0)
                    z_rows(1, 3, 1)
                    unit(5, everything)
                    taps(1)
                    split_in(next_u, next_u % 2, (0, 1))
                    y_rows(0, 0)
                    y_rows(0, 1)
                    y_lo_conv(0, 0)
                    y_lo_conv(0, 1)
                    split_in(next_u, next_u % 2, (2, 3))
                    y_rows(1, 0)
                    y_rows(1, 1)
                    y_lo_conv(1, 0)
                    y_lo_conv(1, 1)
                    split_late_out(s, 2)
                    split_late_out(s, 3)
                else:
                    def rope_products(n):
                        unit, t = divmod(n, 2)
                        heads = NKV if unit == 0 else 8
                        dve.wait_ge(proj_done, 2 * (u + unit) + t + 1)
                        if n < 2:
                            dve.wait_ge(v_ready, n + 1)
                        if n >= 1:
                            dve.wait_ge(rope_out, rope_writes(n))
                        src = proj[t][:, 0:heads * HD].rearrange("p (h d) -> p h d", d=HD // 2)
                        for to, table in ((rope_cos, cos_t), (rope_sin, sin_t)):
                            both = dve.tensor_tensor(to[:, 0:heads * HD].rearrange("p (h d) -> p h d", d=HD // 2), src,
                                                     table[:, t, :].unsqueeze(1).to_broadcast([P, 2 * heads, HD // 2]),
                                                     ALU.mult)
                        both.then_inc(rope_ab, 1)

                    def mask_max(g):
                        t, heads = attention_group(g)
                        keys = W // len(heads)
                        dve.wait_ge(scores_done, g + 1)
                        if g >= 2:
                            dve.wait_ge(probT_ps, g - 1)
                        buf = pair[:, g % 2, :].rearrange("p (h n) -> p h n", n=keys)
                        dve.scalar_tensor_tensor(out=buf, in0=scores[g // 6][g % 2][:, :].rearrange("p (h n) -> p h n", n=keys),
                                                 scalar=1.0 / math.sqrt(HD),
                                                 in1=band[:, 2 * P - keys:2 * P].unsqueeze(1).to_broadcast([P, len(heads), keys]),
                                                 op0=ALU.mult, op1=ALU.add).then_inc(masked, 1)
                        dve.wait_ge(masked, g + 1)
                        hs = slice(heads[0], heads[-1] + 1, 2)
                        dve.tensor_reduce(row_max[:, t, hs], buf, AX.X, ALU.max, negate=True).then_inc(max_step, 1)
                        dve.wait_ge(max_step, g + 1)
                        dve.tensor_tensor(neg_max[:, t, hs], row_max[:, t, hs], neg_sink[:, hs],
                                          ALU.min).then_inc(neg_max_ready, 1)

                    def sink_args(b):
                        half, t = divmod(b, 2)
                        hs = slice(8 * half, 8 * half + 8)
                        dve.wait_ge(neg_max_ready, BATCH_LAST[b] + 1)
                        dve.tensor_tensor(sink_arg[:, t, hs], neg_max[:, t, hs], neg_sink[:, hs],
                                          ALU.subtract).then_inc(sink_arg_ready, 1)

                    def normalise(b):
                        half, t = divmod(b, 2)
                        hs = slice(8 * half, 8 * half + 8)
                        last = BATCH_LAST[b]
                        dve.wait_ge(exp_done, exps_through(last))
                        dve.wait_ge(sink_exp_done, b + 1)
                        dve.tensor_tensor(denom[:, t, hs], prob_sum[:, t, hs], sink_exp[:, t, hs],
                                          ALU.add).then_inc(den_step, 1)
                        dve.wait_ge(den_step, 2 * b + 1)
                        dve.reciprocal(inv_denom[:, t, hs], denom[:, t, hs]).then_inc(den_step, 1)
                        dve.wait_ge(den_step, 2 * b + 2)
                        dve.wait_ge(pv_done, last + 1)
                        if b >= 2:
                            dve.wait_ge(o_ps_T, b - 1)
                        dve.tensor_tensor(o_tok[:, t, :].rearrange("p (h d) -> p h d", d=HD),
                                          o_ps[half][:, :].rearrange("p (h d) -> p h d", d=HD),
                                          inv_denom[:, t, hs].unsqueeze(2).to_broadcast([P, 8, HD]),
                                          ALU.mult).then_inc(o_ready, 1)

                    def y_lo_attn(b):
                        half, t = divmod(b, 2)
                        ks, ts = slice(half * HALF, (half + 1) * HALF), slice(t * P, (t + 1) * P)
                        dve.wait_ge(y_hi_done, 4 + b + 1)
                        dve.tensor_tensor(y_lo[:, ks, ts], tp4[oT_ps[b]], y_hi[:, ks, ts].bitcast(F32),
                                          ALU.subtract).then_inc(y_lo_done, 1)

                    dve.wait_ge(trig_ready, 2)
                    for t in range(NT):
                        dve.wait_ge(rstd_ready, 2 * m + t + 1)
                        for table in (cos_t, sin_t):
                            dve.tensor_scalar(table[:, t, :], table[:, t, :], rstd_col[0][:, t:t + 1], None,
                                              ALU.mult).then_inc(tables_ready, 1)
                    def next_piece(q):
                        split_in(next_u, next_u % 2, (q,))

                    split_in(u + 1, (u + 1) % 2, (0, 1))
                    dve.wait_ge(tables_ready, 4)
                    rope_products(0)
                    split_in(u + 1, (u + 1) % 2, (2, 3))
                    rope_products(1)
                    split_in(u + 2, (u + 2) % 2, range(PIECES))
                    rope_products(2)
                    split_out(o, o % 2)
                    rope_products(3)
                    mask_max(0)
                    mask_max(1)
                    sink_args(0)
                    split_out(o + 1, (o + 1) % 2, (0,))
                    rope_products(4)
                    mask_max(2)
                    split_out(o + 1, (o + 1) % 2, (1,))
                    mask_max(3)
                    normalise(0)
                    next_piece(0)
                    mask_max(4)
                    mask_max(5)
                    y_lo_attn(0)
                    sink_args(1)
                    next_piece(1)
                    rope_products(5)
                    next_piece(2)
                    mask_max(6)
                    normalise(1)
                    mask_max(7)
                    y_lo_attn(1)
                    sink_args(2)
                    mask_max(8)
                    next_piece(3)
                    mask_max(9)
                    normalise(2)
                    split_late_out(s, 2, (0,))
                    y_lo_attn(2)
                    mask_max(10)
                    split_late_out(s, 2, (1,))
                    mask_max(11)
                    sink_args(3)
                    split_late_out(s, 3)
                    normalise(3)
                    y_lo_attn(3)
                for t in range(NT):
                    residual(m + 1, t, 0.5 if kind == FF else 1.0)
                    if s + 1 < len(STAGES):
                        norm_lo(m + 1, t)
            dve.wait_ge(g_fin_landed, 16)
            for t in range(NT):
                i = 2 * len(STAGES) + t
                dve.wait_ge(rstd_ready, i + 1)
                for half in range(2):
                    part = slice(half * W, (half + 1) * W)
                    dve.scalar_tensor_tensor(out=fin[:, t, part], in0=x[:, t, part], scalar=rstd[:, i:i + 1],
                                             in1=g_fin[:, part], op0=ALU.mult, op1=ALU.mult).then_inc(fin_ready, 1)

        @block.tensor
        def _(pe):
            def project(m, u, t, slot, ks=range(KD), first=False, fresh=False):
                if 0 in ks and not first and not fresh:
                    pe.wait_ge(in_lo_done, PIECES * (u + 1))
                for k in ks:
                    if first and k % HALF == 0:
                        pe.wait_ge(xT_lo_done, 4 * m + 2 * t + k // HALF + 1)
                    if (fresh or first and t == 0) and k % 2 == 0:
                        pe.wait_ge(in_lo_done, PIECES * u + k // 2 + 1)
                    x_hi, x_lo = (a[:, k, t * P:(t + 1) * P] for a in (xT_hi, xT_lo))
                    pe.matmul(proj[t][:, :], x_hi, in_hi[:, slot, k, :], start=(k == 0), stop=False)
                    pe.matmul(proj[t][:, :], x_hi, in_lo[:, slot, k, :], start=False, stop=False)
                    last = pe.matmul(proj[t][:, :], x_lo, in_hi[:, slot, k, :], start=False, stop=(k == KD - 1))
                if KD - 1 in ks:
                    last.then_inc(proj_done, 1)

            def down(hi, lo, t, slot, kt, start, stop, passes=(0, 1, 2), late=None, halves=(0, 1)):
                w_hi, w_lo = (out_hi, out_lo) if late is None else (in_hi, in_lo)
                for n in passes:
                    a, w = ((hi, w_hi), (hi, w_lo), (lo, w_hi))[n]
                    for half in halves:
                        if late is None:
                            part = w[:, slot, kt, half * W:(half + 1) * W]
                        else:
                            part = w[:, slot, late_out_at(late, kt) + half, :]
                        last = pe.matmul(acc[t][half][:, :], a, part,
                                         start=(start and n == 0), stop=(stop and n == 2))
                return last

            def down_hidden(c, o, t, h_slot, slot, parts=range(6), start=False, stop=False, halves=(0, 1)):
                for part in parts:
                    kt, n = divmod(part, 3)
                    last = down(*(a[:, h_slot, kt, t * P:(t + 1) * P] for a in (hT_hi, hT_lo)), t, slot, kt,
                                start=(start and kt == 0), stop=(stop and kt == 1), passes=(n,), halves=halves)
                return last

            def down_mixed(s, n, o, t, kts=(0, 1)):
                mix, u_end = int(STAGES[s] == ATTN), IN_BASE[s + 1]
                pe.wait_ge(y_lo_done, 4 * mix + 2 * (n // 2) + t + 1)
                late, slot = (n, (u_end - 1) % 2) if n >= 2 else (None, (o + n) % 2)
                for kt in kts:
                    pe.wait_ge(out_lo_done, 2 * (o + n) + kt + 1)
                    last = down(*(a[:, 2 * n + kt, t * P:(t + 1) * P] for a in (y_hi, y_lo)), t, slot, kt,
                                start=(n == 0 and kt == 0), stop=(n == 3 and kt == 1), late=late)
                return last

            def transpose_x(m, t):
                for half in range(2):
                    if m == 0:
                        pe.wait_ge(x_landed[t], 16)
                    else:
                        pe.wait_ge(x_ready, 4 * (m - 1) + 2 * t + half + 1)
                    if t == 1:
                        pe.wait_ge(gained, 4 * m + half + 1)
                    for n in range(HALF):
                        k = half * HALF + n
                        last = pe.transpose(tp[half][:, n * P:(n + 1) * P], x[:, t, k * P:(k + 1) * P], ident[:, :])
                    last.then_inc(xT_ps, 1)

            def transpose_hidden(c):
                pe.wait_ge(h_ready, 2 * c + 2)
                if not isinstance(c, int) or c >= 1:
                    pe.wait_ge(hT_lo_done, c)
                for kt in range(2):
                    for t in range(NT):
                        last = pe.transpose(tp[0][:, kt * SEQ + t * P:kt * SEQ + (t + 1) * P],
                                            hid_buf[:, t, kt * P:(kt + 1) * P], ident[:, :])
                last.then_inc(hT_ps, 1)

            def transpose_rows(rows_of, bank, done):
                for n in range(HALF):
                    last = pe.transpose(tp[bank][:, n * P:(n + 1) * P], rows_of[:, n * P:(n + 1) * P], ident[:, :])
                last.then_inc(done, 1)

            pe.wait_ge(ident_ready, 2)
            transpose_x(0, 0)
            pe.wait_ge(rows_landed, 16 * (len(gains) + 1))
            n_rows = GAIN_ROWS + CONV_ROWS
            pe.transpose(proj[1][:, 0:n_rows], rows[:, :], ident[0:n_rows, 0:n_rows]).then_inc(cols_ps, 1)
            for _ in range(WARM_UP):
                pe.transpose(acc[0][0][:, 0:P], ident[:, :], ident[:, :])

            for s, kind in enumerate(STAGES):
                u, o, m = IN_BASE[s], OUT_BASE[s], s
                last_stage = s + 1 == len(STAGES)
                project(m, u, 0, u % 2, range(0, HALF), first=True)
                transpose_x(m, 1)
                project(m, u, 0, u % 2, range(HALF, KD), first=True)
                project(m, u, 1, u % 2, first=True)
                if kind == FF:
                    c = NJ * FF_INDEX[s]

                    def middle(j, par, start=False):
                        for t in range(NT):
                            pe.wait_ge(h_ready, 2 * (c + j - 1) + t + 1)
                            project(m, u + j, t, (u + par) % 2, fresh=(start and t == 0))
                            if t == 0:
                                transpose_hidden(c + j - 1)
                        pe.wait_ge(hT_lo_done, c + j)
                        pe.wait_ge(out_lo_done, 2 * (o + j))
                        for t in range(NT):
                            last = down_hidden(c + j - 1, o + j - 1, t, (c + par + 1) % 2, (o + par + 1) % 2, start=start)
                        last.then_inc(out_used, 1)

                    middle(1, 1, start=True)
                    with pe.Fori(0, LOOP_TURNS) as i:
                        for b in range(2):
                            middle(LOOP_FROM + 2 * i + b, b)
                    j = NJ - 1
                    for t in range(NT):
                        pe.wait_ge(h_ready, 2 * (c + j - 1) + t + 1)
                        project(m, u + j, t, (u + j) % 2)
                        if t == 0:
                            transpose_hidden(c + j - 1)
                    pe.wait_ge(hT_lo_done, c + j)
                    pe.wait_ge(out_lo_done, 2 * (o + j))
                    before = (c + j - 1, o + j - 1)
                    slots = ((c + j - 1) % 2, (o + j - 1) % 2)
                    down_hidden(*before, 0, *slots, parts=range(0, 4))
                    transpose_hidden(c + j)
                    down_hidden(*before, 0, *slots, parts=range(4, 6))
                    down_hidden(*before, 1, *slots, parts=range(0, 2))
                    pe.wait_ge(hT_lo_done, c + j + 1)
                    pe.wait_ge(out_lo_done, 2 * (o + j + 1))
                    down_hidden(c + j, o + j, 0, (c + j) % 2, (o + j) % 2, stop=True).then_inc(acc_first, 1)
                    down_hidden(*before, 1, *slots, parts=range(2, 6)).then_inc(out_used, 1)
                    if not last_stage:
                        transpose_x(m + 1, 0)
                    for half in range(2):
                        last = down_hidden(c + j, o + j, 1, (c + j) % 2, (o + j) % 2, stop=True, halves=(half,))
                        if half == 0:
                            last.then_inc(acc_half, 1)
                    last.then_inc(out_used, 1)
                elif kind == CONV:
                    def unit(q, t, *free):
                        for semaphore, count in free:
                            pe.wait_ge(semaphore, count)
                        project(m, u + q, t, (u + q) % 2, fresh=(q == 1 and t == 0))

                    def transpose_z(half, t):
                        pe.wait_ge(z_ready, 2 * half + t + 1)
                        if half == 1:
                            pe.wait_ge(z_feat_ready, t + 1)
                        transpose_rows(z_tok[:, t, :], t, z_ps)

                    def transpose_b(half, t):
                        pe.wait_ge(c_ready, 4 + 2 * half + t + 1)
                        if half == 0:
                            pe.wait_ge(z_feat_ready, 2 + t + 1)
                        else:
                            pe.wait_ge(y_f_ready, t + 1)
                        transpose_rows(c_tok[:, t, :], t, b_ps)

                    unit(1, 0, (c_ready, 1))
                    unit(1, 1, (c_ready, 2))
                    unit(2, 0, (z_ready, 1))
                    transpose_z(0, 0)
                    transpose_z(0, 1)
                    unit(2, 1, (z_ready, 2))
                    unit(3, 0, (c_ready, 3))
                    unit(3, 1, (c_ready, 4))
                    unit(4, 0, (z_ready, 3))
                    transpose_z(1, 0)
                    transpose_z(1, 1)
                    unit(4, 1, (z_ready, 4))
                    unit(5, 0, (c_ready, 5))
                    transpose_b(0, 0)
                    transpose_b(0, 1)
                    unit(5, 1, (c_ready, 6))
                else:
                    def queries(n, t, ks=range(KD)):
                        if 0 in ks:
                            pe.wait_ge(rope_ab, 2 * (n - 1) + t + 1)
                            if n == 1:
                                pe.wait_ge(v_ready, t + 1)
                        project(m, u + n, t, (u + n) % 2, ks, fresh=(n == 1 and t == 0))

                    def transpose_qk(n):
                        pe.wait_ge(rope_out, rope_writes(n + 1))
                        if n >= 2:
                            pe.wait_ge(qkT_ready, n - 1)
                        if n >= 4:
                            pe.wait_ge(y_lo_done, 4 + 1)
                        transpose_rows((kd_tok if n < 2 else q_tok)[:, n % 2, :], n % 2, qk_ps)

                    def score(g):
                        t, heads = attention_group(g)
                        keys = W // len(heads)
                        pe.wait_ge(qkT_ready, 3 + t if g < 6 else 5 + t)
                        if g in (6, 7):
                            pe.wait_ge(rope_ab, g - 1)
                        if g >= 2:
                            pe.wait_ge(masked, g - 1)
                        for n, h in enumerate(heads):
                            ps = slice(HD * (h % 2), HD * (h % 2) + HD)
                            last = pe.matmul(scores[g // 6][g % 2][:, n * keys:(n + 1) * keys],
                                             qT[ps, h // 2, t * P:(t + 1) * P], kT[ps, h // 4, 0:keys],
                                             start=True, stop=True)
                        last.then_inc(scores_done, 1)

                    def transpose_probs(g):
                        pe.wait_ge(exp_done, exps_through(g))
                        if g >= 1:
                            pe.wait_ge(probT_ready, g)
                        if g == 9:
                            pe.wait_ge(y_lo_done, 4 + 3)
                        for n in range(HALF):
                            last = pe.transpose(pT_ps[g // 6][:, n * P:(n + 1) * P], pair[:, g % 2, n * P:(n + 1) * P], ident[:, :])
                        last.then_inc(probT_ps, 1)

                    def values(g):
                        t, heads = attention_group(g)
                        blocks = 1 + t
                        pe.wait_ge(probT_ready, g + 1)
                        if g in (2, 6, 8):
                            pe.wait_ge(o_ready, {2: 1, 6: 2, 8: 3}[g])
                        if g == 6:
                            pe.wait_ge(y_lo_done, 4 + 2)
                        for n, h in enumerate(heads):
                            for b in range(blocks):
                                at = n * blocks + b
                                last = pe.matmul(o_ps[g // 6][:, (h % 8) * HD:(h % 8 + 1) * HD],
                                                 pT[:, g % 2, at * P:(at + 1) * P],
                                                 v_tok[:, b, (h // 4) * HD:(h // 4 + 1) * HD],
                                                 start=(b == 0), stop=(b == blocks - 1))
                        last.then_inc(pv_done, 1)

                    def transpose_o(b):
                        pe.wait_ge(o_ready, b + 1)
                        if b < 2:
                            pe.wait_ge(qkT_ready, 4 if b == 0 else 6)
                        else:
                            pe.wait_ge(probT_ready, 9 if b == 2 else 12)
                        transpose_rows(o_tok[:, b % 2, :], oT_ps[b], o_ps_T)

                    queries(1, 0)
                    transpose_qk(0)
                    transpose_qk(1)
                    queries(1, 1)
                    transpose_qk(2)
                    queries(2, 0, range(0, 2))
                    score(0)
                    score(1)
                    queries(2, 0, range(2, 4))
                    transpose_qk(3)
                    queries(2, 0, range(4, KD))
                    through = (2, 4, 5, 7, 8)
                    for g in range(6):
                        transpose_probs(g)
                        if g < 4:
                            score(g + 2)
                        if g < 5:
                            queries(2, 1, range(through[g - 1] if g > 0 else 0, through[g]))
                        else:
                            pe.wait_ge(masked, 6)
                            down_mixed(s, 0, o, 0, (0,))
                            score(6)
                            score(7)
                        values(g)
                        if g == 2:
                            transpose_o(0)
                        if g == 4:
                            transpose_qk(4)
                    transpose_qk(5)
                    down_mixed(s, 0, o, 0, (1,))
                    shares = {6: [(1, 0, 0)], 7: [(1, 0, 1), (0, 1, 0)], 8: [(0, 1, 1)],
                              9: [(1, 1, 1)], 10: [(2, 0, 0)], 11: [(2, 0, 1)]}
                    for g in range(6, GROUPS):
                        transpose_probs(g)
                        if g == 6:
                            transpose_o(1)
                        if g < 10:
                            score(g + 2)
                        for n, t, kt in shares[g]:
                            last = down_mixed(s, n, o, t, (kt,))
                            if t == 1 and kt == 1:
                                last.then_inc(out_used, 1)
                        values(g)
                        if g == 8:
                            transpose_o(2)
                            down_mixed(s, 1, o, 1, (0,))
                    down_mixed(s, 3, o, 0, (0,))
                    transpose_o(3)
                    down_mixed(s, 3, o, 0, (1,)).then_inc(acc_first, 1)
                    down_mixed(s, 2, o, 1).then_inc(out_used, 1)
                    transpose_x(m + 1, 0)
                    down_mixed(s, 3, o, 1).then_inc(out_used, 1)
                if kind == CONV:
                    for n in range(2):
                        down_mixed(s, n, o, 0)
                        if n == 0:
                            transpose_b(1, 0)
                            transpose_b(1, 1)
                        down_mixed(s, n, o, 1).then_inc(out_used, 1)
                    down_mixed(s, 2, o, 0)
                    down_mixed(s, 3, o, 0).then_inc(acc_first, 1)
                    down_mixed(s, 2, o, 1).then_inc(out_used, 1)
                    transpose_x(m + 1, 0)
                    down_mixed(s, 3, o, 1).then_inc(out_used, 1)


_INS = ["x", "positions", "ln_ff1", "w_ff1_in", "w_ff1_out", "ln_mix", "ln_ff2", "w_ff2_in", "w_ff2_out",
        "conv_w_in", "conv_kernel", "conv_w_out", "attn_w_qkv", "attn_sinks", "attn_w_o", "ln_final"]


def kernel(**inputs):
    import concourse.bacc as bacc
    from concourse.bass_utils import run_bass_kernel_spmd

    nc = bacc.Bacc("TRN2", target_bir_lowering=False, num_devices=1)
    arrays, args = {}, []
    freq = (THETA ** (-np.arange(0, HD, 2, dtype=np.float64) / HD)).astype(np.float32)
    given = {name: np.ascontiguousarray(inputs[name]) for name in _INS}
    given["inv_freq"] = np.ascontiguousarray(np.broadcast_to(freq, (P, HD // 2)))
    for name, a in given.items():
        arrays[f"in_{name}"] = a
        args.append(nc.dram_tensor(f"in_{name}", a.shape, mybir.dt.from_np(a.dtype), kind="ExternalInput").ap())
    args.append(nc.dram_tensor("out_0", (1, SEQ, D), F32, kind="ExternalOutput").ap())
    build(nc, *args)
    r = run_bass_kernel_spmd(nc, [arrays], core_ids=[0])
    return r.results[0]["out_0"]
```
